# Optimizing a Trainium2 kernel written in Bass

```python
import jax, jax.numpy as jnp
from jax import lax
import numpy as np

D_MODEL = 1024
BATCH = 1
SEQ = 1024
DEPTH = 1

D_CONV_A = D_MODEL
D_CONV_B = D_MODEL
K_SHORT = 3
K_CONF = 31
D_IN = 3 * D_CONV_A + 2 * D_CONV_B + 2 * D_MODEL
N_GROUPS = 4
EXPERTS_PER_GROUP = 8
N_EXPERTS = N_GROUPS * EXPERTS_PER_GROUP
TOP_K = 2
D_EXPERT = D_MODEL // 2
BLOCK_ROWS = 128
RMS_EPS = 1e-6
LN_EPS = 1e-5

kernel_name = "hybrid_shortconv_conformer_hmoe_block"

def rmsnorm(x, g):
    xf = x.astype(jnp.float32)
    y = xf * lax.rsqrt(jnp.mean(xf * xf, axis=-1, keepdims=True) + RMS_EPS)
    return (y * g.astype(jnp.float32)).astype(x.dtype)

def layernorm(x, g, b):
    xf = x.astype(jnp.float32)
    mu = jnp.mean(xf, axis=-1, keepdims=True)
    var = jnp.mean(jnp.square(xf - mu), axis=-1, keepdims=True)
    y = (xf - mu) * lax.rsqrt(var + LN_EPS)
    return (y * g.astype(jnp.float32) + b.astype(jnp.float32)).astype(x.dtype)

def depthwise_conv(x, w):
    k = w.shape[0]
    pad = k // 2
    return lax.conv_general_dilated(
        x, w[:, None, :].astype(x.dtype), window_strides=(1,), padding=[(pad, pad)],
        dimension_numbers=("NWC", "WIO", "NWC"), feature_group_count=x.shape[-1])

def mixer_sublayer(h, w_in, conv_a, w_a_out, conv_b, b_conv_b, ln_g, ln_b, w_b_out, w_o):
    z = h @ w_in
    cuts = np.cumsum([D_CONV_A, D_CONV_A, D_CONV_A, D_CONV_B, D_CONV_B, D_MODEL]).tolist()
    b_a, c_a, x_a, u_b, v_b, g_a, g_b = jnp.split(z, cuts, axis=-1)
    y_a = (b_a * depthwise_conv(c_a * x_a, conv_a)) @ w_a_out
    u = u_b * jax.nn.sigmoid(v_b)
    u = depthwise_conv(u, conv_b) + b_conv_b
    u = jax.nn.silu(layernorm(u, ln_g, ln_b))
    y_b = u @ w_b_out
    m = jax.nn.sigmoid(g_a) * y_a + jax.nn.sigmoid(g_b) * y_b
    return m @ w_o

def hier_moe(h, w_rg, b_rg, w_re, b_re, w_gate, w_up, w_down):
    bsz, s, d = h.shape
    xt = h.reshape(-1, d)
    n = xt.shape[0]
    lg = (xt @ w_rg).astype(jnp.float32) + b_rg.astype(jnp.float32)
    pg = jax.nn.softmax(lg, axis=-1)
    g_idx = jnp.argmax(lg, axis=-1)
    g_prob = jnp.take_along_axis(pg, g_idx[:, None], axis=-1)
    le = ((xt @ w_re).astype(jnp.float32) + b_re.astype(jnp.float32)).reshape(
        n, N_GROUPS, EXPERTS_PER_GROUP)
    le = jnp.take_along_axis(le, g_idx[:, None, None], axis=1)[:, 0]
    top_l, top_i = lax.top_k(le, TOP_K)
    top_p = jax.nn.softmax(top_l, axis=-1)
    weight = (g_prob * top_p).reshape(-1)
    expert = (g_idx[:, None] * EXPERTS_PER_GROUP + top_i).reshape(-1).astype(jnp.int32)
    token = jnp.repeat(jnp.arange(n, dtype=jnp.int32), TOP_K)
    order = jnp.argsort(expert)
    e_sorted = expert[order]
    t_sorted = token[order]
    w_sorted = weight[order]
    counts = jnp.bincount(expert, length=N_EXPERTS)
    padded = ((counts + BLOCK_ROWS - 1) // BLOCK_ROWS) * BLOCK_ROWS
    start = jnp.cumsum(counts) - counts
    pend = jnp.cumsum(padded)
    pstart = pend - padded
    rank = jnp.arange(n * TOP_K, dtype=jnp.int32) - start[e_sorted]
    dest = pstart[e_sorted] + rank
    n_rows = ((n * TOP_K + BLOCK_ROWS - 1) // BLOCK_ROWS) * BLOCK_ROWS + N_EXPERTS * BLOCK_ROWS
    n_blocks = n_rows // BLOCK_ROWS
    tok_buf = jnp.zeros((n_rows,), jnp.int32).at[dest].set(t_sorted)
    w_buf = jnp.zeros((n_rows,), jnp.float32).at[dest].set(w_sorted)
    blk_e = jnp.minimum(
        jnp.searchsorted(pend, jnp.arange(n_blocks) * BLOCK_ROWS, side="right"),
        N_EXPERTS - 1).astype(jnp.int32)
    xb = xt[tok_buf].reshape(n_blocks, BLOCK_ROWS, d)

    def expert_block(args):
        xblk, e = args
        a = xblk @ w_gate[e]
        u = xblk @ w_up[e]
        return (jax.nn.silu(a) * u) @ w_down[e]

    yb = lax.map(expert_block, (xb, blk_e)).reshape(n_rows, d)
    yb = yb * w_buf[:, None].astype(yb.dtype)
    out = jnp.zeros_like(xt).at[tok_buf].add(yb)
    return out.reshape(bsz, s, d)

def setup_inputs(seed: int = 0) -> dict:
    key = jax.random.key(seed)
    ks = jax.random.split(key, 24)
    D, L = D_MODEL, DEPTH

    def nrm(k, shape, scale):
        return jax.random.normal(k, shape, jnp.float32) * scale

    return {
        "x": nrm(ks[0], (BATCH, SEQ, D), 1.0),
        "c": nrm(ks[1], (BATCH, D), 1.0),
        "w_ada": nrm(ks[2], (L, D, 6 * D), 0.5 * D ** -0.5),
        "b_ada": nrm(ks[3], (L, 6 * D), 0.02),
        "g_norm1": 1.0 + nrm(ks[4], (L, D), 0.05),
        "w_in": nrm(ks[5], (L, D, D_IN), D ** -0.5),
        "conv_a": nrm(ks[6], (L, K_SHORT, D_CONV_A), K_SHORT ** -0.5),
        "w_a_out": nrm(ks[7], (L, D_CONV_A, D), D_CONV_A ** -0.5),
        "conv_b": nrm(ks[8], (L, K_CONF, D_CONV_B), K_CONF ** -0.5),
        "b_conv_b": nrm(ks[9], (L, D_CONV_B), 0.02),
        "ln_conv_g": 1.0 + nrm(ks[10], (L, D_CONV_B), 0.05),
        "ln_conv_b": nrm(ks[11], (L, D_CONV_B), 0.02),
        "w_b_out": nrm(ks[12], (L, D_CONV_B, D), D_CONV_B ** -0.5),
        "w_o": nrm(ks[13], (L, D, D), D ** -0.5),
        "g_norm2": 1.0 + nrm(ks[14], (L, D), 0.05),
        "w_router_g": nrm(ks[15], (L, D, N_GROUPS), D ** -0.5),
        "b_router_g": nrm(ks[16], (L, N_GROUPS), 0.01),
        "w_router_e": nrm(ks[17], (L, D, N_EXPERTS), D ** -0.5),
        "b_router_e": nrm(ks[18], (L, N_EXPERTS), 0.01),
        "w_gate": nrm(ks[19], (L, N_EXPERTS, D, D_EXPERT), D ** -0.5),
        "w_up": nrm(ks[20], (L, N_EXPERTS, D, D_EXPERT), D ** -0.5),
        "w_down": nrm(ks[21], (L, N_EXPERTS, D_EXPERT, D), D_EXPERT ** -0.5),
        "g_final": 1.0 + nrm(ks[22], (D,), 0.05),
    }

def reference(x, c, w_ada, b_ada, g_norm1, w_in, conv_a, w_a_out, conv_b, b_conv_b,
              ln_conv_g, ln_conv_b, w_b_out, w_o, g_norm2, w_router_g, b_router_g,
              w_router_e, b_router_e, w_gate, w_up, w_down, g_final):
    for l in range(DEPTH):
        mod = jax.nn.silu(c) @ w_ada[l] + b_ada[l]
        sh1, sc1, gt1, sh2, sc2, gt2 = jnp.split(mod[:, None, :], 6, axis=-1)
        h = rmsnorm(x, g_norm1[l]) * (1.0 + sc1) + sh1
        x = x + gt1 * mixer_sublayer(h, w_in[l], conv_a[l], w_a_out[l], conv_b[l], b_conv_b[l],
                                     ln_conv_g[l], ln_conv_b[l], w_b_out[l], w_o[l])
        h = rmsnorm(x, g_norm2[l]) * (1.0 + sc2) + sh2
        x = x + gt2 * hier_moe(h, w_router_g[l], b_router_g[l], w_router_e[l], b_router_e[l],
                               w_gate[l], w_up[l], w_down[l])
    return rmsnorm(x, g_final)


_drawn_inputs = setup_inputs


def setup_inputs(seed=0):
    import zlib

    import numpy as np

    out = dict(_drawn_inputs(seed))
    spreads = {}
    factors = {'b_conv_b': 8.0,
     'ln_conv_g': 6.513,
     'ln_conv_b': 8.0,
     'g_norm2': 3.245,
     'b_router_g': 8.0,
     'b_router_e': 6.962}
    for name, (base, spread) in spreads.items():
        noise = np.random.default_rng([zlib.crc32(name.encode()), seed]).standard_normal(out[name].shape)
        drawn = base * np.exp(spread * noise) if base else spread * noise
        out[name] = __import__('jax').numpy.asarray(drawn.astype(out[name].dtype))
    for name, factor in factors.items():
        out[name] = (out[name] * factor).astype(out[name].dtype)
    return out
```

```python
from contextlib import ExitStack

import numpy as np

import concourse.bass as bass
from concourse import mybir

F32 = mybir.dt.float32
F32R = mybir.dt.float32r
I32 = mybir.dt.int32
ALU = mybir.AluOpType
ACT = mybir.ActivationFunctionType
AX_X = mybir.AxisListType.X

P = 128
RMS_EPS = 1e-6
LN_EPS = 1e-5
NEG = -3.0e38

KINDS = ["conf_gate", "conf_value", "short_c", "short_x", "short_b", "gate_a", "gate_b"]
W_IN_GROUP = {"short_b": 0, "short_c": 1, "short_x": 2, "conf_value": 3, "conf_gate": 4, "gate_a": 5, "gate_b": 6}
NK = len(KINDS)
W_SLOT = [0, 1, 2, 0, 1, 2, 1]
W_TURN = [0, 0, 0, 1, 1, 1, 2]
W_BACK = [4, 2, 4, 3, 3, 3, 2]
W_PER_ROUND = [2, 3, 2]
PS_SLOT = [0, 1, 2, 3, 0, 1, 2]

ROW_CONV_A, ROW_BIAS_B, ROW_LN_G, ROW_LN_B, ROW_G1, ROW_SH, ROW_SC, ROW_C = 31, 34, 35, 36, 37, 38, 39, 40
N_ROWS = 41

CREDIT_SLAB = NK
CREDIT_ACT_EVAC = 4
CREDIT_DVE_EVAC = 3
CREDIT_FREE = 1
CREDIT_STORE = 2
CREDIT_DOWN = 2


def slab_turn(n):
    j = n - 8 * NK
    slot = j % 3
    before = [8 * NK - 4, 8 * NK - 1, 8 * NK - 2][j] if j < 3 else n - 3
    return slot, 8 * W_PER_ROUND[slot] + j // 3, before


def encoder_block(nc, x, c, w_ada, b_ada, g_norm1, w_in, conv_a, w_a_out, conv_b, b_conv_b, ln_g, ln_b,
                  w_b_out, w_o, g_norm2, w_rg, b_rg, w_re, b_re, w_gate, w_up, w_down, g_final, out):
    S, D = x.shape
    KT = D // P
    NT = S // P
    H = S // 2
    KB, KA = conv_b.shape[0], conv_a.shape[0]
    PAD_B, PAD_A = KB // 2, KA // 2
    NG = w_rg.shape[1]
    NE = w_re.shape[1]
    EPG = NE // NG
    F = w_gate.shape[2]
    FT = F // P
    PAIRS = 2 * S
    NBLK = PAIRS // P + NE
    NR = NG + NE
    assert D == S == 1024 and KT == 8 and NT == 8 and F == 512 and NBLK % 2 == 0

    with ExitStack() as ctx:
        base = (nc.sbuf_base + 63) // 64 * 64

        def at(name, offset, shape, dtype):
            return nc.alloc_sbuf_tensor_at(name, shape, dtype, offset=base + offset)

        T4 = 4 * D
        oA, oAl, oB, oBl = 0, 8 * T4, 16 * T4, 24 * T4
        oW = 32 * T4
        oS = oW + 9 * T4
        oR = oS + 4 * T4
        oM = oR + 4 * T4

        A_hi = at("A_hi", oA, [P, KT, S], F32R)
        A_lo = at("A_lo", oAl, [P, KT, S], F32R)
        B_hi = at("B_hi", oB, [P, KT, S], F32R)
        B_lo = at("B_lo", oBl, [P, KT, S], F32R)
        xn = at("xn", oB, [P, NT, D], F32)
        xnT = at("xnT", oAl, [P, KT, S], F32)
        conf = at("conf", oB, [P, KT * S], F32)
        conf_sq = at("conf_sq", oBl, [P, KT, S], F32)
        prow = at("prow", oBl, [P, D], F32)
        macc1 = at("macc1", oBl + T4, [P, 2, D], F32)
        hsc = at("hsc", oBl + 6 * T4, [P, 2, S], F32)
        junk0 = at("junk0", oBl + 5 * T4, [P, D], F32)
        sig_v = at("sig_v", oBl, [P, S], F32)
        c_sb = at("c_sb", oBl + T4, [P, S], F32)
        cx = at("cx", oBl + 2 * T4, [P, S + 2 * PAD_A], F32)
        conv_acc_a = at("conv_acc_a", oBl + 3 * T4 + 32, [P, S], F32)
        conv_acc_b = at("conv_acc_b", oBl + 4 * T4 + 32, [P, S], F32)
        gate_st = at("gate_st", oBl + 5 * T4 + 32, [P, 2, S], F32)
        w_raw = at("w_raw", oW, [P, 3, KT * P], F32)
        w_hi = at("w_hi", oW + 3 * T4, [P, 3, KT * P], F32R)
        w_lo = at("w_lo", oW + 6 * T4, [P, 3, KT * P], F32R)
        stream = at("stream", oS, [P, 4, D], F32)
        rows = at("rows", oR, [P, 4, D], F32)
        GT1, SH2, A2, GT2 = range(4)
        top = [oM]

        def small(name, shape, dtype=F32):
            n = int(np.prod(shape[1:])) * 4
            t = at(name, top[0], shape, dtype)
            top[0] += (n + 31) // 32 * 32
            return t

        glu_w = S + 2 * PAD_B
        glu = small("glu", [P, glu_w])
        s1 = at("s1", oM, [P, S], F32)
        s2 = small("s2", [P, S])
        ident = small("ident", [P, P])
        ones = small("ones", [P, P])
        mean_w = small("mean_w", [P, P])
        cols = small("cols", [P, KT, N_ROWS])
        colc = small("colc", [P, N_ROWS])
        modc = small("modc", [P, 2, KT])
        a1 = small("a1", [P, KT])
        sig_c = small("sig_c", [P, KT])
        ss = small("ss", [P, NT])
        rstd = small("rstd", [P, NT])
        msq, root, newt = small("msq", [P, NT]), small("root", [P, NT]), small("newton", [P, NT])
        assert base + top[0] <= nc.sbuf_usable_end, (base + top[0], nc.sbuf_usable_end)

        junk3 = at("junk3", oW, [P, D], F32)
        h2 = at("h2", oW + T4, [P, 2, D], F32)
        w_r = at("w_r", oW + 3 * T4, [P, KT, NR], F32)
        b_r = at("b_r", oW + 3 * T4 + 2048, [P, NR], F32)
        logits = at("logits", oW + 3 * T4 + 4096, [P, NT, NR], F32)
        tri = at("tri", oW + 3 * T4 + 8192, [P, P], F32)
        onesr = ones
        ro = [oW + 3 * T4 + 8192 + 512]

        def rt(name, shape, dtype=F32):
            n = int(np.prod(shape[1:])) * 4
            t = at(name, ro[0], shape, dtype)
            ro[0] += (n + 31) // 32 * 32
            assert ro[0] <= oS
            return t

        iota_g = rt("iota_g", [P, NT, NG])
        iota_e = rt("iota_e", [P, NT, EPG])
        thr = rt("thr", [P, NT])
        blk_no = rt("blk_no", [P, NBLK])
        gsm = rt("gsm", [P, 8, NT])
        oh_g = rt("oh_g", [P, NT, NG])
        tg = rt("tg", [P, NT, NG])
        te = rt("te", [P, NT, EPG])
        le = rt("le", [P, NT, EPG])
        oh_k = rt("oh_k", [P, 2, NT, EPG])
        big = rt("big", [P, NT, NE])
        e_k = rt("e_k", [P, 2, NT, NE])
        mask = rt("mask", [P, NT, NE])
        cum = rt("cum", [P, NT + 1, NE])
        nb_e = rt("nb_e", [P, NE])
        pend = rt("pend", [P, 2, NE])
        posf = rt("posf", [P, 2, NT])
        cmp_nb = rt("cmp_nb", [P, NE, NT])
        cmp_b = rt("cmp_b", [1, NBLK, NE])

        tab = at("tab", oM, [1, 64], I32)
        posi = at("posi", oM + 256, [P, 2, NT], I32)
        pair_id = at("pair_id", oM + 512, [P, NT, 2, 2], I32)
        w_tok = at("w_tok", oM + 768, [P, 2, NT], F32)
        tabf = at("tabf", oM + 1024, [1, 64], F32)
        idx_all = at("idx_all", oM + 1280, [P, NBLK + 1, 2], I32)
        fill = at("fill", oM + 2048, [P, (NBLK + 1) * 2], I32)
        g_idx = at("g_idx", oM + 2560, [P, 2], I32)
        s_idx = at("s_idx", oM + 2592, [P, 2], I32)
        hT_hi = at("hT_hi", oM + 4224, [P, FT, P], F32R)
        hT_lo = at("hT_lo", oM + 4224 + 2048, [P, FT, P], F32R)

        NCH = 6
        C8 = 2 * D
        e_raw = at("e_raw", 0, [P, NCH, C8], F32)
        e_hi = at("e_hi", NCH * 4 * C8, [P, NCH, C8], F32R)
        e_lo = at("e_lo", 2 * NCH * 4 * C8, [P, NCH, C8], F32R)
        oX = 3 * NCH * 4 * C8
        xg = at("xg", oX, [P, 2, D], F32)
        xT_hi = at("xT_hi", oX + 2 * T4, [P, 2, KT * P], F32R)
        xT_lo = at("xT_lo", oX + 4 * T4, [P, 2, KT * P], F32R)
        y_sb = at("y_sb", oX + 6 * T4, [P, 2, D], F32)
        sg = at("sg", oX + 8 * T4, [P, 2, F // 2], F32)
        hid = at("hid", oX + 8 * T4 + 2048, [P, 2, F // 2], F32)
        assert oX + 8 * T4 + 4096 <= oR

        NF = 3
        f_y = [at("f_y0", 4 * 4 * C8, [P, 2, D], F32), at("f_y1", 5 * 4 * C8, [P, 2, D], F32),
               at("f_y2", (NCH + 4) * 4 * C8, [P, 2, D], F32)]
        f_x = at("f_x", (NCH + 5) * 4 * C8, [P, 2, D], F32)
        f_x2 = at("f_x2", (2 * NCH + 4) * 4 * C8, [P, D], F32)
        f_t = at("f_t", (2 * NCH + 4) * 4 * C8 + T4, [P, D], F32)
        f_o = at("f_o", (2 * NCH + 5) * 4 * C8, [P, 2, D], F32)
        f_xs = [f_x[:, 0, :], f_x[:, 1, :], f_x2[:]]

        ps = ctx.enter_context(nc.psum_tensor("ps", [P, 4, S], F32))

        def dram(name, shape, dtype=F32):
            return nc.dram_tensor(name, shape, dtype, kind="Internal").ap()

        d_a = dram("d_short", [D, S])
        d_g = [dram("d_gate_a", [D, S]), dram("d_gate_b", [D, S])]
        d_ma = dram("d_ma", [D, S])
        d_x1 = dram("d_x1", [S, D])
        d_h2 = dram("d_h2", [S, D])
        d_y = dram("d_y", [PAIRS, D])
        d_pos = dram("d_pos", [(NBLK + 1) * P, 2], I32)

        def sem(name):
            return ctx.enter_context(nc.semaphore(name))

        s_par, s_const, s_fill = sem("params_in"), sem("const_ready"), sem("const_steps")
        s_rows_in, s_g2_in, s_wr_in = sem("bias_rows_in"), sem("gfin_in"), sem("router_in")
        st_full = [sem(f"stream_full{i}") for i in range(4)]
        st_free = [sem(f"stream_free{i}") for i in range(4)]
        wr_full = [sem(f"w_raw_full{i}") for i in range(3)]
        w_hi_done, w_lo_done, pe_slab = sem("w_hi_done"), sem("w_lo_done"), sem("pe_slab")
        act_evac, dve_evac = sem("act_evac"), sem("dve_evac")
        dv = sem("dve_step")
        dvl = sem("dve_loop_step")
        s_parT, s_cols, s_sigc, s_cs = sem("parT"), sem("cols_ready"), sem("sig_c_ready"), sem("silu_c_ready")
        s_ssq, s_rstd, s_xn, s_xT, s_xTev = sem("ssq"), sem("rstd_x"), sem("xn_ready"), sem("xT_ps"), sem("xnT_ready")
        s_macc, s_modc, s_h, s_hhi, s_hlo = sem("macc1_ready"), sem("modc_ps"), sem("h_f32"), sem("h_hi"), sem("h_lo")
        sp_a, sp_g = sem("short_spilled"), [sem("gate_a_spilled"), sem("gate_b_spilled")]
        s_ahi, s_alo = sem("short_hi"), sem("short_lo")
        s_conf, s_mean, s_cent, s_sq, s_var = sem("conf_ready"), sem("mean_ps"), sem("centred"), sem("squared"), sem("var_ps")
        s_ln, s_lsig, s_sw, s_bhi, s_blo = sem("ln_t"), sem("ln_sig"), sem("swish"), sem("conf_hi"), sem("conf_lo")
        ev2 = sem("evac_out")
        s_ma, sp_ma = sem("ma_ready"), sem("ma_spilled")
        s_m, s_mhi, s_mlo = sem("m_f32"), sem("m_hi"), sem("m_lo")
        s_bc, s_bcev, s_bcdv = sem("rows_ps"), sem("rows_act"), sem("rows_dve")
        s_ohi, s_olo = sem("wo_hi"), sem("wo_lo")
        pe_o, s_x1, s_ss3, s_r3, s_h2 = sem("pe_o"), sem("x1_ready"), sem("ssq3"), sem("rstd3"), sem("h2_ready")
        sp_x1, sp_h2, s_h2T, s_h2Tc, s_lg, s_lgev = (sem("x1_spilled"), sem("h2_spilled"), sem("h2T_ps"), sem("h2T_sb"),
                                                     sem("logits_ps"), sem("logits_sb"))
        s_exp, s_mask, s_rank, s_tab, s_pos = sem("exp_ready"), sem("mask_ready"), sem("rank_ps"), sem("tab_ready"), sem("pos_ready")
        s_e = sem("exp_in")
        s_posd, s_tabin, s_dfill = sem("pos_stored"), sem("idx_in"), sem("pos_table_filled")
        e_full = [sem(f"expert_full{i}") for i in range(NCH)]
        gu_hi, gu_lo, gu_used = sem("gu_hi"), sem("gu_lo"), sem("gu_used")
        d_hi, d_lo, d_used = sem("down_hi"), sem("down_lo"), sem("down_used")
        s_xz, xg_full = sem("xg_zeroed"), [sem("xg_full0"), sem("xg_full1")]
        t_done, xThi, xTlo = sem("xT_done"), sem("xT_hi_done"), sem("xT_lo_done")
        gu0, sgd, hd0, hd1, a_h = sem("gu0_done"), sem("sg_done"), sem("hid0_done"), sem("hid1_done"), sem("hid_half")
        ht_ps, ht_hi, ht_lo = sem("hT_ps"), sem("hT_hi_done"), sem("hT_lo_done")
        y_ev, y_st, h2_free, p_step, p_copy, moe_done = sem("y_evac"), sem("y_stored"), sem("h2_free"), sem("pool_step"), sem("pool_copy"), sem("moe_done")
        f_full, f_free = [sem(f"f_full{i}") for i in range(NF)], sem("f_free")
        f_s0, f_x2s, f_ssq, f_r, f_out, f_st = (sem("f_scaled"), sem("f_x2"), sem("f_ssq"), sem("f_rstd"), sem("f_out"), sem("f_stored"))
        a_free, g_free, y_free = sem("short_free"), [sem("gate_a_free"), sem("gate_b_free")], sem("y_free")
        dve_held, act_held, pe_held = sem("dve_held"), sem("act_held"), sem("pe_held")
        sp_step = sem("sync_step")
        s_msq, s_root = sem("mean_square"), sem("root")
        s_lnv, s_lnr = sem("ln_var"), sem("ln_root")

        block = ctx.enter_context(nc.Block())

        M_X, M_ADA1 = 0, NT
        M_ADA2 = M_ADA1 + 2 * KT
        M_A = M_ADA2 + 4 * KT
        M_GA = M_A + KT
        M_GB = M_GA + KT
        M_G2 = M_GB + 2 * KT
        M_WO = M_G2 + 1
        M_XR = M_WO + KT

        def tile(m):
            return stream[:, m % 4, :]

        def load_tile(sp, m, src):
            if m >= 4:
                sp.wait_ge(st_free[m % 4], m // 4)
            sp.dma_start(tile(m), src).then_inc(st_full[m % 4], 16)

        def wait_tile(eng, m):
            eng.wait_ge(st_full[m % 4], 16 * (m // 4 + 1))

        def slab_in(kind, ch):
            col = W_IN_GROUP[kind] * D
            return w_in[:, bass.ds(ch * P + col, P)].rearrange("(k p) n -> p k n", p=P)

        def slab_out(n):
            j = n - NK * KT
            w = w_a_out if j < KT else w_b_out
            return w[:, j % KT * P:(j % KT + 1) * P].rearrange("(k p) n -> p k n", p=P)

        raw3 = w_raw[:].rearrange("p s (k n) -> p s k n", k=KT)

        @block.sync
        def _(sp):
            def held(s, value):
                sp.wait_ge(s, value)
                sp.sem_inc(sp_step, 1)

            for src, r, n in ((conv_b, 0, KB), (conv_a, ROW_CONV_A, KA), (b_conv_b, ROW_BIAS_B, 1), (ln_g, ROW_LN_G, 1),
                              (ln_b, ROW_LN_B, 1), (g_norm1, ROW_G1, 1), (b_ada[0:2], ROW_SH, 2), (c, ROW_C, 1)):
                sp.dma_start(prow[r:r + n, :], src).then_inc(s_par, 16)
            for i in range(NT):
                load_tile(sp, M_X + i, x[i * P:(i + 1) * P, :])
            for k in range(KT):
                for q in range(2):
                    load_tile(sp, M_ADA1 + 2 * k + q, w_ada[k * P:(k + 1) * P, q * D:(q + 1) * D])
            sp.wait_ge(s_const, 1)
            sp.dma_start(rows[0:1, :, :], b_ada[2:6].unsqueeze(0)).then_inc(s_rows_in, 16)

            sp.wait_ge(s_cols, 2)
            with sp.Fori(0, KT) as ch:
                for kind in range(NK):
                    s = W_SLOT[kind]
                    held(w_lo_done, ch * NK + (kind - W_BACK[kind] + 1 + CREDIT_SLAB))
                    sp.dma_start(raw3[:, s], slab_in(KINDS[kind], ch)).then_inc(wr_full[s], 16)
                    if kind in (0, 2, 4, 5):
                        q = (0, 2, 4, 5).index(kind)
                        held(st_free[q], ch + M_ADA2 // 4)
                        sp.dma_start(stream[:, q, :], w_ada[bass.ds(ch * P, P), (2 + q) * D:(3 + q) * D]).then_inc(st_full[q], 16)

            def load_slab(n):
                slot, _, before = slab_turn(n)
                sp.wait_ge(w_lo_done, before + 1 + CREDIT_SLAB)
                sp.dma_start(raw3[:, slot], slab_out(n)).then_inc(wr_full[slot], 16)

            n0 = NK * KT
            for n in range(n0, n0 + 3):
                load_slab(n)
            sp.wait_ge(sp_a, 16 * KT)
            for k in range(KT):
                load_tile(sp, M_A + k, d_a[k * P:(k + 1) * P, :])
            sp.wait_ge(sp_g[0], 16 * KT)
            for j in range(KT):
                load_tile(sp, M_GA + j, d_g[0][j * P:(j + 1) * P, :])
                load_slab(n0 + 3 + j)
            sp.wait_ge(sp_g[1], 16 * KT)
            for j in range(KT):
                load_tile(sp, M_GB + 2 * j, d_g[1][j * P:(j + 1) * P, :])
                sp.wait_ge(sp_ma, 16 * (j + 1))
                load_tile(sp, M_GB + 2 * j + 1, d_ma[j * P:(j + 1) * P, :])
                if j < KT - 3:
                    load_slab(n0 + KT + 3 + j)
            load_tile(sp, M_G2, g_norm2.partition_broadcast(P).rearrange("p a n -> p (a n)"))
            for k in range(KT):
                load_tile(sp, M_WO + k, w_o[k * P:(k + 1) * P, :])
            for i in range(NT):
                load_tile(sp, M_XR + i, x[i * P:(i + 1) * P, :])
                if i == 0:
                    sp.wait_ge(pe_slab, n0 + 2 * KT + CREDIT_SLAB)
                    sp.dma_start(w_r[:, :, 0:NG], w_rg.rearrange("(k p) n -> p k n", p=P)).then_inc(s_wr_in, 16)
                    sp.dma_start(w_r[:, :, NG:NR], w_re.rearrange("(k p) n -> p k n", p=P)).then_inc(s_wr_in, 16)
                    sp.dma_start(b_r[:, 0:NG], b_rg.partition_broadcast(P).rearrange("p a n -> p (a n)")).then_inc(s_wr_in, 16)
                    sp.dma_start(b_r[:, NG:NR], b_re.partition_broadcast(P).rearrange("p a n -> p (a n)")).then_inc(s_wr_in, 16)

            sp.wait_ge(s_tab, 1)

            def load_gu(blk, q, e):
                for part, w in ((0, w_gate), (1, w_up)):
                    dst = e_raw[:, q, :].rearrange("p (k w n) -> p k w n", k=2, w=2)[:, :, part, :]
                    src = w[bass.ds(e, 1), 2 * q * P:2 * (q + 1) * P, :].rearrange("a (k p) n -> p (a k) n", p=P)
                    sp.dma_start(dst, src).then_inc(e_full[q], 16)

            n_blk = sp.value_load(tab[0:1, NBLK:NBLK + 1], min_val=1, max_val=NBLK - 1)
            e0 = sp.value_load(tab[0:1, 0:1], min_val=0, max_val=NE - 1)
            for q in range(4):
                load_gu(0, q, e0)
            with sp.Fori(0, NBLK) as b:
                with sp.If(b < n_blk):
                    e = sp.value_load(tab[0:1, bass.ds(b, 1)], min_val=0, max_val=NE - 1)
                    for q in range(2):
                        held(d_lo, b * 2 + (q - 1 + CREDIT_DOWN))
                        src = w_down[bass.ds(e, 1), 2 * q * P:2 * (q + 1) * P, :].rearrange("a (k p) n -> p (a k) n", p=P)
                        sp.dma_start(e_raw[:, 4 + q, :].rearrange("p (k n) -> p k n", k=2), src).then_inc(e_full[4 + q], 16)
                    e_next = sp.value_load(tab[0:1, bass.ds(b + 1, 1)], min_val=0, max_val=NE - 1)
                    for q in range(4):
                        held(gu_lo, b * 4 + (q + 1))
                        load_gu(b + 1, q, e_next)

            sp.wait_ge(moe_done, 1)
            sp.dma_start(rows[:, SH2, :], g_final.partition_broadcast(P).rearrange("p a n -> p (a n)")).then_inc(s_g2_in, 16)
            for i in range(NT):
                if i >= NF:
                    sp.wait_ge(f_free, i - NF + 1)
                y_rows = d_y[2 * i * P:2 * (i + 1) * P, :].rearrange("(p k) n -> p k n", k=2)
                sp.dma_start(f_y[i % NF][:], y_rows).then_inc(f_full[i % NF], 16)
                sp.dma_start(f_xs[i % NF], d_x1[i * P:(i + 1) * P, :]).then_inc(f_full[i % NF], 16)
                if i >= 1:
                    sp.wait_ge(f_out, i)
                    sp.dma_start(out[(i - 1) * P:i * P, :], f_o[:, (i - 1) % 2, :]).then_inc(f_st, 16)
            sp.wait_ge(f_out, NT)
            sp.dma_start(out[(NT - 1) * P:NT * P, :], f_o[:, (NT - 1) % 2, :]).then_inc(f_st, 16)
            sp.wait_ge(f_st, 16 * NT)

        @block.gpsimd
        def _(pool):
            g = nc.gpsimd
            steps = [0]

            def step(ins):
                steps[0] += 1
                ins.then_inc(s_fill, 1)
                pool.wait_ge(s_fill, steps[0])

            def held(s, value):
                pool.wait_ge(s, value)
                pool.sem_inc(p_step, 1)

            g.memset(ones[:], 1.0)
            g.memset(mean_w[:], 1.0 / D)
            step(g.memset(ident[:], 0.0))
            step(g.affine_select(out=ident[:], in_=ident[:], compare_op=ALU.not_equal, fill=1.0, base=0,
                                 pattern=[[-1, P]], channel_multiplier=1))
            g.memset(rows[:], 0.0).then_inc(s_const, 1)
            pool.wait_ge(s_const, 1)

            pool.wait_ge(s_cols, 2)
            with pool.Fori(0, KT) as ch:
                held(dve_evac, ch * 3 + (3 + CREDIT_DVE_EVAC))
                pool.dma_start(d_a[bass.ds(ch * P, P), :], conv_acc_a[:]).then_inc(sp_a, 16)
                for q in range(2):
                    held(act_evac, ch * 4 + (3 + q + CREDIT_ACT_EVAC))
                    pool.dma_start(d_g[q][bass.ds(ch * P, P), :], gate_st[:, q, :]).then_inc(sp_g[q], 16)
                for spilled, free in ((sp_a, a_free), (sp_g[0], g_free[0]), (sp_g[1], g_free[1])):
                    pool.wait_ge(spilled, ch * 16 + 16)
                    pool.sem_inc(free, 1)
            for j in range(KT):
                pool.wait_ge(s_ma, j + 1)
                pool.dma_start(d_ma[j * P:(j + 1) * P, :], tile(M_GA + j)).then_inc(sp_ma, 16)
                pool.wait_ge(sp_ma, 16 * (j + 1))
                pool.sem_inc(st_free[(M_GA + j) % 4], 1)

            pool.wait_ge(pe_slab, NK * KT + 2 * KT + CREDIT_SLAB)
            pool.wait_ge(w_lo_done, NK * KT + 2 * KT + CREDIT_SLAB)
            step(g.affine_select(out=tri[:], in_=ones[:], compare_op=ALU.is_gt, fill=0.0, base=0,
                                 pattern=[[1, P]], channel_multiplier=-1))
            g.iota(iota_g[:], pattern=[[0, NT], [1, NG]], base=0, channel_multiplier=0, allow_small_or_imprecise_dtypes=True)
            g.iota(iota_e[:], pattern=[[0, NT], [1, EPG]], base=0, channel_multiplier=0, allow_small_or_imprecise_dtypes=True)
            g.iota(thr[:], pattern=[[P, NT]], base=0, channel_multiplier=0, allow_small_or_imprecise_dtypes=True)
            g.iota(blk_no[:], pattern=[[1, NBLK]], base=0, channel_multiplier=0, allow_small_or_imprecise_dtypes=True)
            step(g.memset(cum[:, 0, :], 0.0))
            pool.sem_inc(s_const, 1)

            for i in range(NT):
                pool.wait_ge(s_x1, i + 1)
                pool.dma_start(d_x1[i * P:(i + 1) * P, :], tile(M_XR + i)).then_inc(sp_x1, 16)
                pool.wait_ge(s_h2, i + 1)
                pool.dma_start(d_h2[i * P:(i + 1) * P, :], h2[:, i % 2, :]).then_inc(sp_h2, 16)
                pool.wait_ge(sp_x1, 16 * (i + 1))
                pool.sem_inc(st_free[(M_XR + i) % 4], 1)
                pool.wait_ge(sp_h2, 16 * (i + 1))
                pool.sem_inc(h2_free, 1)

            for k in range(2):
                g.iota(pair_id[:, :, k, 0:1], pattern=[[P, NT]], base=0, channel_multiplier=1)
                g.iota(pair_id[:, :, k, 1:2], pattern=[[2 * P, NT]], base=k, channel_multiplier=2)
            step(g.memset(fill[:], 4 * PAIRS))
            pool.dma_start(d_pos.rearrange("(p b) t -> p (b t)", p=P), fill[:]).then_inc(s_dfill, 16)

            pool.wait_ge(s_pos, 1)
            step(g.memset(xg[:], 0.0))
            pool.wait_ge(s_dfill, 16)
            for k in range(2):
                for i in range(NT):
                    g.indirect_dma_start(d_pos, bass.IndirectOffsetOnAxis(ap=posi[:, k, i:i + 1], axis=0),
                                         pair_id[:, i, k, :], None, bounds_check=NBLK * P - 1,
                                         oob_is_err=False).then_inc(s_posd, 16)
            pool.wait_ge(s_posd, 16 * PAIRS // P)
            pool.dma_start(idx_all[:], d_pos.rearrange("(b p) t -> p b t", p=P)).then_inc(s_tabin, 16)
            pool.wait_ge(s_tabin, 16)

            def gather(slot, blk, copies):
                g.tensor_copy(g_idx[:, slot:slot + 1], idx_all[:, bass.ds(blk, 1), 0:1].rearrange("p a t -> p (a t)")).then_inc(p_copy, 1)
                held(p_copy, copies)
                g.indirect_dma_start(xg[:, slot, :], None, d_h2, bass.IndirectOffsetOnAxis(ap=g_idx[:, slot:slot + 1], axis=0),
                                     bounds_check=S - 1, oob_is_err=False).then_inc(xg_full[slot], 16)

            n_blk = pool.value_load(tab[0:1, NBLK:NBLK + 1], min_val=1, max_val=NBLK - 1)
            gather(0, 0, 1)
            with pool.Fori(0, NBLK // 2) as pair:
                for s in range(2):
                    with pool.If(pair * 2 + s < n_blk):
                        b = pair * 2 + s
                        held(t_done, b + 1)
                        gather(1 - s, b + 1, b * 2 + 2)
                        g.tensor_copy(s_idx[:, s:s + 1], idx_all[:, bass.ds(b, 1), 1:2].rearrange("p a t -> p (a t)")).then_inc(p_copy, 1)
                        held(p_copy, b * 2 + 3)
                        held(y_ev, b + 2)
                        g.indirect_dma_start(d_y, bass.IndirectOffsetOnAxis(ap=s_idx[:, s:s + 1], axis=0), y_sb[:, s, :], None,
                                             bounds_check=PAIRS - 1, oob_is_err=False).then_inc(y_st, 16)
                        pool.wait_ge(y_st, b * 16 + 16)
                        pool.sem_inc(y_free, 1)
            pool.sem_inc(moe_done, 1)

        @block.scalar
        def _(act):
            a = nc.scalar
            def take_root(stage, i):
                act.wait_ge(s_msq, stage * NT + i + 1)
                a.activation(root[:, i:i + 1], msq[:, i:i + 1], ACT.Sqrt).then_inc(s_root, 1)

            act.wait_ge(s_cols, 1)
            a.activation(sig_c[:], cols[:, :, ROW_C], ACT.Sigmoid).then_inc(s_sigc, 1)
            for i in range(NT):
                wait_tile(act, M_X + i)
                a.activation(junk0[:], tile(M_X + i), ACT.Square, accum_out=ss[:, i:i + 1]).then_inc(s_ssq, 1)
                take_root(0, i)
                act.wait_ge(s_rstd, i + 1)
                a.activation(xn[:, i, :], tile(M_X + i), ACT.Copy, scale=rstd[:, i:i + 1]).then_inc(s_xn, 1)
                act.wait_ge(s_xn, i + 1)
                act.sem_inc(st_free[(M_X + i) % 4], 1)
            act.sem_inc(act_evac, CREDIT_ACT_EVAC)
            for q in range(2):
                act.sem_inc(g_free[q], CREDIT_FREE)
            for k in range(KT):
                act.wait_ge(s_h, k + 1)
                a.copy(A_hi[:, k, :], hsc[:, k % 2, :]).then_inc(s_hhi, 1)

            def split(n, slot, full, before):
                act.wait_ge(wr_full[slot], full)
                act.wait_ge(pe_slab, before)
                a.copy(w_hi[:, slot, :], w_raw[:, slot, :]).then_inc(w_hi_done, 1)

            act.wait_ge(s_cols, 2)
            for kind in range(2):
                split(kind, W_SLOT[kind], 16, CREDIT_SLAB)
            with act.Fori(0, KT) as ch:
                for kind in range(NK):
                    name = KINDS[kind]
                    src = ps[:, PS_SLOT[kind], :]
                    n_done = ch * NK + (kind + 1 + CREDIT_SLAB)
                    if name == "conf_gate":
                        act.wait_ge(dve_evac, ch * 3 + (1 - 3 + CREDIT_DVE_EVAC))
                        act.wait_ge(pe_slab, n_done)
                        a.activation(sig_v[:], src, ACT.Sigmoid).then_inc(act_evac, 1)
                    if name == "short_c":
                        act.wait_ge(dve_evac, ch * 3 + (2 - 3 + CREDIT_DVE_EVAC))
                        act.wait_ge(pe_slab, n_done)
                        a.copy(c_sb[:], src).then_inc(act_evac, 1)
                    if name in ("gate_a", "gate_b"):
                        q = 0 if name == "gate_a" else 1
                        act.wait_ge(g_free[q], ch + CREDIT_FREE)
                        act.wait_ge(pe_slab, n_done)
                        a.activation(gate_st[:, q, :], src, ACT.Sigmoid).then_inc(act_evac, 1)
                    k2, over = (kind + 2) % NK, (kind + 2) // NK
                    s = W_SLOT[k2]
                    split(None, s, ch * (16 * W_PER_ROUND[s]) + 16 * (over * W_PER_ROUND[s] + W_TURN[k2] + 1),
                          ch * NK + (kind + 2 - W_BACK[k2] + 1 + CREDIT_SLAB))

            n0 = NK * KT
            for k in range(KT):
                wait_tile(act, M_A + k)
                act.wait_ge(pe_slab, n0 + CREDIT_SLAB)
                a.copy(A_hi[:, k, :], tile(M_A + k)).then_inc(s_ahi, 1)

            def split2(n):
                if n < n0 + 2 * KT:
                    slot, turn, before = slab_turn(n)
                    split(n, slot, 16 * (turn + 1), before + 1 + CREDIT_SLAB)

            def swish_in(k):
                act.wait_ge(s_ln, k + 1)
                if k >= 1:
                    act.wait_ge(s_sw, k)
                a.activation(s1[:], conf[:, k * S:(k + 1) * S], ACT.Sigmoid, scale=cols[:, k, ROW_LN_G:ROW_LN_G + 1],
                             bias=cols[:, k, ROW_LN_B:ROW_LN_B + 1]).then_inc(s_lsig, 1)

            def conf_hi(k):
                act.wait_ge(s_sw, k + 1)
                a.copy(B_hi[:, k, :], s2[:]).then_inc(s_bhi, 1)

            for j in range(KT):
                split2(n0 + j + 2)
                if j == 1:
                    for spilled in (sp_a, sp_g[0], sp_g[1]):
                        act.wait_ge(spilled, 16 * KT)
                    for k in range(KT):
                        act.wait_ge(s_cent, k + 1)
                        a.activation(conf_sq[:, k, :], conf[:, k * S:(k + 1) * S], ACT.Square).then_inc(s_sq, 1)
                if j == 4:
                    act.wait_ge(s_lnv, 1)
                    a.activation(s1[:], ps[:, 3, :], ACT.Sqrt).then_inc(s_lnr, 1)
                for k in {4: [0, 1], 5: [2, 3], 6: [4, 5], 7: [6, 7]}.get(j, []):
                    swish_in(k)
                    conf_hi(k)
            for j in range(KT):
                act.wait_ge(s_m, j + 1)
                a.copy(A_hi[:, j, :], s2[:]).then_inc(s_mhi, 1)
                split2(n0 + KT + j + 2)
                if j == 1:
                    for q, slot in ((GT1, 2), (SH2, 3)):
                        act.wait_ge(s_bc, q + 1)
                        a.copy(rows[:, q, :], ps[:, slot, :]).then_inc(s_bcev, 1)
                if j == 3:
                    act.wait_ge(s_bc, 4)
                    a.copy(rows[:, GT2, :], ps[:, 3, :]).then_inc(s_bcev, 1)
            for k in range(KT):
                wait_tile(act, M_WO + k)
                act.wait_ge(pe_slab, n0 + 2 * KT + CREDIT_SLAB)
                a.copy(B_hi[:, k, :], tile(M_WO + k)).then_inc(s_ohi, 1)

            def h2_copy(i):
                act.wait_ge(s_h2T, i + 1)
                if i >= 1:
                    act.wait_ge(s_lg, i)
                a.copy(s2[:], ps[:, 2, :]).then_inc(s_h2Tc, 1)

            for i in range(NT):
                act.wait_ge(s_x1, i + 1)
                a.activation(junk3[:], tile(M_XR + i), ACT.Square, accum_out=ss[:, i:i + 1]).then_inc(s_ss3, 1)
                take_root(1, i)
                if i >= 1:
                    h2_copy(i - 1)
            h2_copy(NT - 1)
            act.wait_ge(s_e, 1)
            a.activation(tg[:], tg[:], ACT.Exp).then_inc(s_exp, 1)
            act.wait_ge(s_e, 2)
            a.activation(gsm[:, 5, :], gsm[:, 4, :], ACT.Exp).then_inc(s_exp, 1)
            a.activation(sig_c[0:1, 0:1], ones[0:1, 0:1], ACT.Sigmoid)

            act.sem_inc(y_ev, 1)
            act.sem_inc(y_free, CREDIT_STORE)
            act.wait_ge(s_tab, 1)

            def gu_split(q, full, before):
                act.wait_ge(e_full[q], full)
                if before is not None:
                    act.wait_ge(gu_used, before)
                a.copy(e_hi[:, q, :], e_raw[:, q, :]).then_inc(gu_hi, 1)

            def x_hi(slot, value):
                act.wait_ge(t_done, value)
                a.copy(xT_hi[:, slot, :], ps[:, 1, :]).then_inc(xThi, 1)

            n_blk = act.value_load(tab[0:1, NBLK:NBLK + 1], min_val=1, max_val=NBLK - 1)
            x_hi(0, 2)
            for q in range(4):
                gu_split(q, 32, None)
            with act.Fori(0, NBLK // 2) as pair:
                for s in range(2):
                    with act.If(pair * 2 + s < n_blk):
                        b = pair * 2 + s
                        for q in range(2):
                            act.wait_ge(e_full[4 + q], b * 16 + 16)
                            act.wait_ge(d_used, b * 2 + (q - 1 + CREDIT_DOWN))
                            a.copy(e_hi[:, 4 + q, :], e_raw[:, 4 + q, :]).then_inc(d_hi, 1)
                        act.wait_ge(gu0, b + 1)
                        a.activation(sg[:, 0, :], ps[:, 0, 0:F // 2], ACT.Sigmoid).then_inc(sgd, 1)
                        gu_split(0, b * 32 + 64, b * 4 + 1)
                        act.wait_ge(gu_used, b * 4 + 4)
                        a.activation(sg[:, 1, :], ps[:, 0, F:F + F // 2], ACT.Sigmoid).then_inc(sgd, 1)
                        act.wait_ge(ht_ps, b * 2 + 1)
                        a.copy(hT_hi[:, 0:2, :], ps[:, 3, 0:2 * P]).then_inc(ht_hi, 1)
                        x_hi(1 - s, b + 3)
                        gu_split(1, b * 32 + 64, b * 4 + 2)
                        act.wait_ge(ht_ps, b * 2 + 2)
                        a.copy(hT_hi[:, 2:4, :], ps[:, 3, 4 * P:6 * P]).then_inc(ht_hi, 1)
                        gu_split(2, b * 32 + 64, b * 4 + 3)
                        gu_split(3, b * 32 + 64, b * 4 + 4)
                        act.wait_ge(d_used, b * 2 + (2 + CREDIT_DOWN))
                        act.wait_ge(y_free, b + (CREDIT_STORE - 1))
                        a.copy(y_sb[:, s, :], ps[:, 2, :]).then_inc(y_ev, 1)

            for i in range(NT):
                act.wait_ge(f_full[i % NF], 32 * (i // NF + 1))
                a.activation(f_y[i % NF][:, 0, :], f_y[i % NF][:, 0, :], ACT.Copy, scale=w_tok[:, 0, i:i + 1]).then_inc(f_s0, 1)
                act.wait_ge(f_x2s, i + 1)
                a.activation(f_y[i % NF][:, 0, :], f_t[:], ACT.Square, accum_out=ss[:, i:i + 1]).then_inc(f_ssq, 1)
                take_root(2, i)

        @block.vector
        def _(dve):
            v = nc.vector
            steps = [0]

            def step(ins):
                steps[0] += 1
                ins.then_inc(dv, 1)
                dve.wait_ge(dv, steps[0])

            def held(s, value):
                dve.wait_ge(s, value)
                dve.sem_inc(dve_held, 1)

            dve.wait_ge(s_parT, 1)
            v.tensor_copy(cols[:], ps[:, 2, 0:KT * N_ROWS]).then_inc(s_cols, 1)
            dve.wait_ge(s_cols, 1)
            dve.wait_ge(s_sigc, 1)
            step(v.tensor_tensor(cols[:, :, ROW_C], cols[:, :, ROW_C], sig_c[:], ALU.mult))

            def rms(stage, i):
                n = stage * NT + i + 1
                m, r, t = msq[:, i:i + 1], rstd[:, i:i + 1], newt[:, i:i + 1]
                v.tensor_scalar(m, ss[:, i:i + 1], 1.0 / D, RMS_EPS, ALU.mult, ALU.add).then_inc(s_msq, 1)
                dve.wait_ge(s_msq, n)
                dve.wait_ge(s_root, n)
                step(v.reciprocal(r, root[:, i:i + 1]))
                step(v.scalar_tensor_tensor(t, r, m, r, ALU.mult, ALU.mult))
                step(v.tensor_scalar(t, t, -0.5, 1.5, ALU.mult, ALU.add))
                return v.tensor_tensor(r, r, t, ALU.mult)

            def xT_evac(i):
                dve.wait_ge(s_xT, i + 1)
                v.tensor_copy(xnT[:, :, i * P:(i + 1) * P], ps[:, i % 2, :].rearrange("p (k n) -> p k n", k=KT)).then_inc(s_xTev, 1)

            for i in range(NT):
                dve.wait_ge(s_ssq, i + 1)
                rms(0, i).then_inc(s_rstd, 1)
                if i >= 1:
                    xT_evac(i - 1)
            xT_evac(NT - 1)
            for k in range(KT):
                for q in range(2):
                    m = M_ADA1 + 2 * k + q
                    wait_tile(dve, m)
                    if k == 0:
                        ins = v.tensor_scalar(macc1[:, q, :], tile(m), cols[:, k, ROW_C:ROW_C + 1], None, ALU.mult)
                    else:
                        ins = v.scalar_tensor_tensor(macc1[:, q, :], tile(m), cols[:, k, ROW_C:ROW_C + 1], macc1[:, q, :],
                                                     ALU.mult, ALU.add)
                    step(ins)
                    dve.sem_inc(st_free[m % 4], 1)
            dve.sem_inc(s_macc, 1)
            dve.wait_ge(s_modc, 1)
            step(v.tensor_tensor(modc[:], ps[:, 3, 0:2 * KT].rearrange("p (q k) -> p q k", q=2),
                                 cols[:, :, ROW_SH:ROW_SC + 1].rearrange("p k q -> p q k"), ALU.add))
            step(v.scalar_tensor_tensor(a1[:], modc[:, 1, :], 1.0, cols[:, :, ROW_G1], ALU.add, ALU.mult))
            v.memset(glu[:, 0:PAD_B], 0.0)
            v.memset(glu[:, PAD_B + S:], 0.0)
            v.memset(cx[:, 0:PAD_A], 0.0)
            step(v.memset(cx[:, PAD_A + S:], 0.0))
            dve.wait_ge(s_xTev, NT)
            for k in range(KT):
                if k >= 2:
                    dve.wait_ge(s_hlo, k - 1)
                v.tensor_scalar(hsc[:, k % 2, :], xnT[:, k, :], a1[:, k:k + 1], modc[:, 0, k:k + 1], ALU.mult, ALU.add).then_inc(s_h, 1)
                dve.wait_ge(s_h, k + 1)
                dve.wait_ge(s_hhi, k + 1)
                v.tensor_tensor(A_lo[:, k, :], hsc[:, k % 2, :], A_hi[:, k, :].bitcast(F32), ALU.subtract).then_inc(s_hlo, 1)
            dve.sem_inc(dve_evac, CREDIT_DVE_EVAC)
            dve.sem_inc(w_lo_done, CREDIT_SLAB)
            dve.sem_inc(a_free, CREDIT_FREE)
            dve.sem_inc(s_cols, 1)
            dve.wait_ge(s_rows_in, 16)

            def split(slot, n_hi):
                dve.wait_ge(w_hi_done, n_hi)
                v.tensor_tensor(w_lo[:, slot, :], w_raw[:, slot, :], w_hi[:, slot, :].bitcast(F32), ALU.subtract).then_inc(w_lo_done, 1)

            for kind in range(2):
                split(W_SLOT[kind], kind + 1)

            TAPS = {1: range(0, 5), 2: range(5, 11), 3: range(11, 15), 4: range(15, 21), 5: range(21, 26), 6: range(26, KB)}
            N_STEPS = 1 + 4 + KB - 1 + KA
            with dve.Fori(0, KT) as ch:
                count = [0]

                def lstep(ins):
                    count[0] += 1
                    ins.then_inc(dvl, 1)
                    dve.wait_ge(dvl, ch * N_STEPS + count[0])

                for kind in range(NK):
                    name = KINDS[kind]
                    src = ps[:, PS_SLOT[kind], :]
                    n_done = ch * NK + (kind + 1 + CREDIT_SLAB)
                    if kind == 0:
                        lstep(v.tensor_copy(colc[:], cols[:, bass.ds(ch, 1), :].rearrange("p a n -> p (a n)")))
                    if name == "conf_value":
                        dve.wait_ge(act_evac, ch * 4 + (1 + CREDIT_ACT_EVAC))
                        dve.wait_ge(pe_slab, n_done)
                        v.tensor_tensor(glu[:, PAD_B:PAD_B + S], src, sig_v[:], ALU.mult).then_inc(dve_evac, 1)
                        dve.wait_ge(dve_evac, ch * 3 + (1 + CREDIT_DVE_EVAC))
                    if name == "short_x":
                        dve.wait_ge(act_evac, ch * 4 + (2 + CREDIT_ACT_EVAC))
                        dve.wait_ge(pe_slab, n_done)
                        v.tensor_tensor(cx[:, PAD_A:PAD_A + S], src, c_sb[:], ALU.mult).then_inc(dve_evac, 1)
                        dve.wait_ge(dve_evac, ch * 3 + (2 + CREDIT_DVE_EVAC))
                        dve.wait_ge(a_free, ch + CREDIT_FREE)
                        for t in range(KA):
                            w = colc[:, ROW_CONV_A + t:ROW_CONV_A + t + 1]
                            if t == 0:
                                lstep(v.tensor_scalar(conv_acc_a[:], cx[:, t:t + S], w, None, ALU.mult))
                            else:
                                lstep(v.scalar_tensor_tensor(conv_acc_a[:], cx[:, t:t + S], w, conv_acc_a[:], ALU.mult, ALU.add))
                    if name == "short_b":
                        dve.wait_ge(pe_slab, n_done)
                        v.tensor_tensor(conv_acc_a[:], src, conv_acc_a[:], ALU.mult).then_inc(dve_evac, 1)
                    k2 = (kind + 2) % NK
                    split(W_SLOT[k2], ch * NK + (kind + 3))
                    if kind in (0, 2, 4, 6):
                        q = kind // 2
                        dve.wait_ge(st_full[q], ch * 16 + 16 * (M_ADA2 // 4 + 1))
                        lstep(v.scalar_tensor_tensor(rows[:, q, :], stream[:, q, :], colc[:, ROW_C:ROW_C + 1], rows[:, q, :],
                                                     ALU.mult, ALU.add))
                        dve.sem_inc(st_free[q], 1)
                    for t in TAPS.get(kind, []):
                        w = colc[:, t:t + 1]
                        if t == 0:
                            lstep(v.tensor_scalar(conv_acc_b[:], glu[:, t:t + S], w, colc[:, ROW_BIAS_B:ROW_BIAS_B + 1], ALU.mult, ALU.add))
                        elif t < KB - 1:
                            lstep(v.scalar_tensor_tensor(conv_acc_b[:], glu[:, t:t + S], w, conv_acc_b[:], ALU.mult, ALU.add))
                        else:
                            v.scalar_tensor_tensor(conf[:, bass.ds(ch * S, S)], glu[:, t:t + S], w, conv_acc_b[:],
                                                   ALU.mult, ALU.add).then_inc(s_conf, 1)
                            held(s_conf, ch + 1)
                assert count[0] == N_STEPS, count

            n0 = NK * KT
            for k in range(KT):
                dve.wait_ge(s_ahi, k + 1)
                v.tensor_tensor(A_lo[:, k, :], tile(M_A + k), A_hi[:, k, :].bitcast(F32), ALU.subtract).then_inc(s_alo, 1)
                dve.wait_ge(s_alo, k + 1)
                dve.sem_inc(st_free[(M_A + k) % 4], 1)

            def split2(n):
                if n < n0 + 2 * KT:
                    split(slab_turn(n)[0], n + 1)

            def ln_t(k):
                u = conf[:, k * S:(k + 1) * S]
                v.tensor_tensor(u, ps[:, 3, :], u, ALU.mult).then_inc(s_ln, 1)

            def swish(k):
                u = conf[:, k * S:(k + 1) * S]
                dve.wait_ge(s_lsig, k + 1)
                step(v.tensor_scalar(u, u, cols[:, k, ROW_LN_G:ROW_LN_G + 1], cols[:, k, ROW_LN_B:ROW_LN_B + 1], ALU.mult, ALU.add))
                if k >= 1:
                    dve.wait_ge(s_blo, k)
                v.tensor_tensor(s2[:], u, s1[:], ALU.mult).then_inc(s_sw, 1)
                if k + 1 < KT:
                    ln_t(k + 1)
                dve.wait_ge(s_bhi, k + 1)
                v.tensor_tensor(B_lo[:, k, :], s2[:], B_hi[:, k, :].bitcast(F32), ALU.subtract).then_inc(s_blo, 1)

            for j in range(KT):
                dve.wait_ge(pe_slab, n0 + j + 1 + CREDIT_SLAB)
                wait_tile(dve, M_GA + j)
                v.tensor_tensor(tile(M_GA + j), ps[:, j % 2, :], tile(M_GA + j), ALU.mult).then_inc(s_ma, 1)
                split2(n0 + j + 2)
                if j == 1:
                    dve.wait_ge(s_mean, 1)
                    for k in range(KT):
                        u = conf[:, k * S:(k + 1) * S]
                        v.scalar_tensor_tensor(u, ps[:, 2, :], -1.0, u, ALU.mult, ALU.add).then_inc(s_cent, 1)
                if j == 4:
                    dve.wait_ge(s_cent, KT)
                    dve.wait_ge(s_var, 1)
                    v.tensor_scalar(ps[:, 3, :], ps[:, 3, :], LN_EPS, None, ALU.add).then_inc(s_lnv, 1)
                    dve.wait_ge(s_lnv, 1)
                    dve.wait_ge(s_lnr, 1)
                    step(v.reciprocal(s1[:], s1[:]))
                    step(v.tensor_tensor(s2[:], s1[:], s1[:], ALU.mult))
                    step(v.tensor_tensor(s2[:], s2[:], ps[:, 3, :], ALU.mult))
                    step(v.tensor_scalar(s2[:], s2[:], -0.5, 1.5, ALU.mult, ALU.add))
                    step(v.tensor_tensor(ps[:, 3, :], s1[:], s2[:], ALU.mult))
                    ln_t(0)
                for k in {4: [0, 1], 5: [2, 3], 6: [4, 5], 7: [6, 7]}.get(j, []):
                    swish(k)
            for j in range(KT):
                mg, mm = M_GB + 2 * j, M_GB + 2 * j + 1
                dve.wait_ge(pe_slab, n0 + KT + j + 1 + CREDIT_SLAB)
                wait_tile(dve, mg)
                step(v.tensor_tensor(s1[:], ps[:, j % 2, :], tile(mg), ALU.mult))
                dve.sem_inc(ev2, 1)
                dve.sem_inc(st_free[mg % 4], 1)
                wait_tile(dve, mm)
                if j >= 1:
                    dve.wait_ge(s_mlo, j)
                else:
                    dve.wait_ge(s_blo, KT)
                v.tensor_tensor(s2[:], s1[:], tile(mm), ALU.add).then_inc(s_m, 1)
                dve.wait_ge(s_m, j + 1)
                dve.sem_inc(st_free[mm % 4], 1)
                dve.wait_ge(s_mhi, j + 1)
                v.tensor_tensor(A_lo[:, j, :], s2[:], A_hi[:, j, :].bitcast(F32), ALU.subtract).then_inc(s_mlo, 1)
                split2(n0 + KT + j + 2)
                if j == 3:
                    dve.wait_ge(s_bc, A2 + 1)
                    step(v.tensor_copy(rows[:, A2, :], ps[:, 2, :]))
                    dve.sem_inc(s_bcdv, 1)
            wait_tile(dve, M_G2)
            step(v.scalar_tensor_tensor(rows[:, A2, :], rows[:, A2, :], 1.0, tile(M_G2), ALU.add, ALU.mult))
            dve.sem_inc(st_free[M_G2 % 4], 1)
            for k in range(KT):
                dve.wait_ge(s_ohi, k + 1)
                v.tensor_tensor(B_lo[:, k, :], tile(M_WO + k), B_hi[:, k, :].bitcast(F32), ALU.subtract).then_inc(s_olo, 1)
                dve.wait_ge(s_olo, k + 1)
                dve.sem_inc(st_free[(M_WO + k) % 4], 1)
            dve.wait_ge(s_bcev, 3)

            def logits_evac(i):
                dve.wait_ge(s_lg, i + 1)
                dve.wait_ge(s_wr_in, 64)
                v.tensor_tensor(logits[:, i, :], ps[:, 3, 0:NR], b_r[:], ALU.add).then_inc(s_lgev, 1)

            for i in range(NT):
                xt = tile(M_XR + i)
                dve.wait_ge(pe_o, i + 1)
                step(v.tensor_tensor(s1[:], ps[:, i % 2, :], rows[:, GT1, :], ALU.mult))
                dve.sem_inc(ev2, 1)
                wait_tile(dve, M_XR + i)
                v.tensor_tensor(xt, s1[:], xt, ALU.add).then_inc(s_x1, 1)
                if i >= 2:
                    logits_evac(i - 2)
                dve.wait_ge(s_ss3, i + 1)
                step(rms(1, i))
                if i >= 2:
                    dve.wait_ge(h2_free, i - 1)
                    dve.wait_ge(s_h2T, i - 1)
                hh = h2[:, i % 2, :]
                step(v.scalar_tensor_tensor(hh, xt, rstd[:, i:i + 1], rows[:, A2, :], ALU.mult, ALU.mult))
                v.tensor_tensor(hh, hh, rows[:, SH2, :], ALU.add).then_inc(s_h2, 1)
            logits_evac(NT - 2)
            logits_evac(NT - 1)
            dve.wait_ge(s_lgev, NT)
            dve.wait_ge(s_const, 2)

            def bc(ap, shape):
                return ap.to_broadcast(shape)

            def row(r):
                return gsm[:, r, :]

            def one_hot(dst, values, best, iota, width, tmp):
                shape = [P, NT, width]
                step(v.tensor_tensor(tmp, values, bc(best.unsqueeze(2), shape), ALU.is_equal))
                step(v.scalar_tensor_tensor(tmp, tmp, -1.0e3, iota, ALU.mult, ALU.add))
                step(v.tensor_reduce(row(2), tmp, AX_X, ALU.min))
                step(v.tensor_scalar(row(2), row(2), 1.0e3, None, ALU.add))
                step(v.tensor_tensor(dst, iota, bc(row(2).unsqueeze(2), shape), ALU.is_equal))

            lg, lexp = logits[:, :, 0:NG], logits[:, :, NG:NR]
            step(v.tensor_reduce(row(0), lg, AX_X, ALU.max))
            step(v.tensor_tensor(tg[:], lg, bc(row(0).unsqueeze(2), [P, NT, NG]), ALU.subtract))
            dve.sem_inc(s_e, 1)
            dve.wait_ge(s_exp, 1)
            step(v.tensor_reduce(row(1), tg[:], AX_X, ALU.add))
            step(v.reciprocal(row(1), row(1)))
            one_hot(oh_g[:], lg, row(0), iota_g[:], NG, tg[:])
            b4 = big[:].rearrange("p i (g e) -> p i g e", g=NG)
            step(v.tensor_tensor(b4, lexp.rearrange("p i (g e) -> p i g e", g=NG), bc(oh_g[:].unsqueeze(3), [P, NT, NG, EPG]), ALU.mult))
            step(v.tensor_reduce(le[:], big[:].rearrange("p i (g e) -> p i e g", g=NG), AX_X, ALU.add))
            step(v.tensor_reduce(row(3), le[:], AX_X, ALU.max))
            one_hot(oh_k[:, 0], le[:], row(3), iota_e[:], EPG, te[:])
            step(v.tensor_scalar(te[:], oh_k[:, 0], -1.0, 1.0, ALU.mult, ALU.add))
            step(v.tensor_tensor(le[:], le[:], te[:], ALU.mult))
            step(v.scalar_tensor_tensor(le[:], oh_k[:, 0], NEG, le[:], ALU.mult, ALU.add))
            step(v.tensor_reduce(row(4), le[:], AX_X, ALU.max))
            one_hot(oh_k[:, 1], le[:], row(4), iota_e[:], EPG, te[:])
            step(v.tensor_tensor(row(4), row(4), row(3), ALU.subtract))
            dve.sem_inc(s_e, 1)
            for k in range(2):
                e4 = e_k[:, k].rearrange("p i (g e) -> p i g e", g=NG)
                step(v.tensor_copy(e4, bc(oh_g[:].unsqueeze(3), [P, NT, NG, EPG])))
                step(v.tensor_tensor(e4, e4, bc(oh_k[:, k].unsqueeze(2), [P, NT, NG, EPG]), ALU.mult))
            step(v.tensor_tensor(mask[:], e_k[:, 0], e_k[:, 1], ALU.add))
            for i in range(NT):
                step(v.tensor_tensor(cum[:, i + 1, :], cum[:, i, :], mask[:, i, :], ALU.add))
            dve.sem_inc(s_mask, 1)
            dve.wait_ge(s_exp, 2)
            step(v.tensor_scalar(row(6), row(5), 1.0, None, ALU.add))
            step(v.reciprocal(row(6), row(6)))
            step(v.tensor_tensor(w_tok[:, 0, :], row(6), row(1), ALU.mult))
            step(v.tensor_tensor(w_tok[:, 1, :], w_tok[:, 0, :], row(5), ALU.mult))
            dve.wait_ge(s_rank, 1)
            cnt = ps[:, 0, H:H + NE]
            step(v.tensor_copy(nb_e[:], cnt))
            step(v.tensor_tensor(cmp_nb[:], bc(nb_e[:].unsqueeze(2), [P, NE, NT]), bc(thr[:].unsqueeze(1), [P, NE, NT]), ALU.is_gt))
            step(v.tensor_reduce(nb_e[:], cmp_nb[:], AX_X, ALU.add))
            step(v.tensor_copy(pend[:, 0, :], nb_e[:]))
            cur, shift = 0, 1
            while shift < NE:
                step(v.tensor_copy(pend[:, 1 - cur, 0:shift], pend[:, cur, 0:shift]))
                step(v.tensor_tensor(pend[:, 1 - cur, shift:], pend[:, cur, shift:], pend[:, cur, 0:NE - shift], ALU.add))
                cur, shift = 1 - cur, 2 * shift
            step(v.tensor_tensor(cmp_b[:], bc(pend[0:1, cur, :].unsqueeze(1), [1, NBLK, NE]),
                                 bc(blk_no[0:1].unsqueeze(2), [1, NBLK, NE]), ALU.is_le))
            step(v.memset(tabf[:], 0.0))
            step(v.tensor_reduce(tabf[:, 0:NBLK], cmp_b[:], AX_X, ALU.add))
            step(v.tensor_scalar(tabf[:, 0:NBLK], tabf[:, 0:NBLK], float(NE - 1), None, ALU.min))
            step(v.tensor_copy(tabf[:, NBLK:NBLK + 1], pend[0:1, cur, NE - 1:NE]))
            v.tensor_copy(tab[:], tabf[:]).then_inc(s_tab, 1)
            step(v.tensor_tensor(nb_e[:], pend[:, cur, :], nb_e[:], ALU.subtract))
            step(v.scalar_tensor_tensor(mask[:], bc(nb_e[:].unsqueeze(1), [P, NT, NE]), float(P),
                                        ps[:, 0, 0:NT * NE].rearrange("p (i e) -> p i e", i=NT), ALU.mult, ALU.add))
            for k in range(2):
                step(v.tensor_tensor(e_k[:, k], e_k[:, k], mask[:], ALU.mult))
                step(v.tensor_reduce(posf[:, k, :], e_k[:, k], AX_X, ALU.add))
            v.tensor_copy(posi[:], posf[:]).then_inc(s_pos, 1)

            for s, n in ((d_lo, CREDIT_DOWN), (ht_lo, CREDIT_DOWN), (hd0, 1), (hd1, 1)):
                dve.sem_inc(s, n)

            def gu_split(q, value):
                dve.wait_ge(gu_hi, value)
                v.tensor_tensor(e_lo[:, q, :], e_raw[:, q, :], e_hi[:, q, :].bitcast(F32), ALU.subtract).then_inc(gu_lo, 1)

            def x_lo(slot, value):
                dve.wait_ge(xThi, value)
                v.tensor_tensor(xT_lo[:, slot, :], ps[:, 1, :], xT_hi[:, slot, :].bitcast(F32), ALU.subtract).then_inc(xTlo, 1)

            def hidden(half, n_sg, n_ah, done):
                dve.wait_ge(sgd, n_sg)
                pair_ps = ps[:, 0, half * F:(half + 1) * F]
                v.tensor_tensor(hid[:, half, :], pair_ps[:, 0:F // 2], sg[:, half, :], ALU.mult).then_inc(a_h, 1)
                dve.wait_ge(a_h, n_ah)
                v.tensor_tensor(hid[:, half, :], pair_ps[:, F // 2:F], hid[:, half, :], ALU.mult).then_inc(done, 1)

            def h_lo(half, value):
                dve.wait_ge(ht_hi, value)
                v.tensor_tensor(hT_lo[:, 2 * half:2 * half + 2, :], ps[:, 3, half * 4 * P:half * 4 * P + 2 * P],
                                hT_hi[:, 2 * half:2 * half + 2, :].bitcast(F32), ALU.subtract).then_inc(ht_lo, 1)

            n_blk = dve.value_load(tab[0:1, NBLK:NBLK + 1], min_val=1, max_val=NBLK - 1)
            x_lo(0, 1)
            for q in range(4):
                gu_split(q, q + 1)
            with dve.Fori(0, NBLK // 2) as pair:
                for s in range(2):
                    with dve.If(pair * 2 + s < n_blk):
                        b = pair * 2 + s
                        for q in range(2):
                            dve.wait_ge(d_hi, b * 2 + (q + 1))
                            v.tensor_tensor(e_lo[:, 4 + q, :], e_raw[:, 4 + q, :], e_hi[:, 4 + q, :].bitcast(F32),
                                            ALU.subtract).then_inc(d_lo, 1)
                        hidden(0, b * 2 + 1, b * 2 + 1, hd0)
                        gu_split(0, b * 4 + 5)
                        hidden(1, b * 2 + 2, b * 2 + 2, hd1)
                        h_lo(0, b * 2 + 1)
                        x_lo(1 - s, b + 2)
                        gu_split(1, b * 4 + 6)
                        h_lo(1, b * 2 + 2)
                        gu_split(2, b * 4 + 7)
                        gu_split(3, b * 4 + 8)

            base_steps = steps[0]
            for i in range(NT):
                y, xr = f_y[i % NF], f_xs[i % NF]
                dve.wait_ge(f_full[i % NF], 32 * (i // NF + 1))
                dve.wait_ge(f_s0, i + 1)
                step(v.scalar_tensor_tensor(y[:, 1, :], y[:, 1, :], w_tok[:, 1, i:i + 1], y[:, 0, :], ALU.mult, ALU.add))
                step(v.tensor_tensor(y[:, 1, :], y[:, 1, :], rows[:, GT2, :], ALU.mult))
                v.tensor_tensor(f_t[:], y[:, 1, :], xr, ALU.add).then_inc(f_x2s, 1)
                dve.wait_ge(f_x2s, i + 1)
                dve.wait_ge(f_ssq, i + 1)
                dve.sem_inc(f_free, 1)
                step(rms(2, i))
                dve.wait_ge(s_g2_in, 16)
                if i >= 2:
                    dve.wait_ge(f_st, 16 * (i - 1))
                v.scalar_tensor_tensor(f_o[:, i % 2, :], f_t[:], rstd[:, i:i + 1], rows[:, SH2, :], ALU.mult, ALU.mult).then_inc(f_out, 1)
                dve.wait_ge(f_out, i + 1)

        @block.tensor
        def _(pe):
            t = nc.tensor

            def three(dst, st_hi, st_lo, mv_hi, mv_lo, first, last):
                t.matmul(dst, st_hi, mv_hi, start=first, stop=False)
                t.matmul(dst, st_hi, mv_lo, start=False, stop=False)
                return t.matmul(dst, st_lo, mv_hi, start=False, stop=last)

            pe.wait_ge(s_fill, 2)
            pe.wait_ge(s_par, 16 * 8)
            for k in range(KT):
                last = t.transpose(ps[:, 2, k * N_ROWS:(k + 1) * N_ROWS], prow[0:N_ROWS, k * P:(k + 1) * P], ident[0:N_ROWS, 0:N_ROWS])
            last.then_inc(s_parT, 1)
            for i in range(NT):
                pe.wait_ge(s_xn, i + 1)
                if i >= 2:
                    pe.wait_ge(s_xTev, i - 1)
                for k in range(KT):
                    last = t.transpose(ps[:, i % 2, k * P:(k + 1) * P], xn[:, i, k * P:(k + 1) * P], ident[:])
                last.then_inc(s_xT, 1)
            pe.wait_ge(s_macc, 1)
            pe.wait_ge(s_const, 1)
            for q in range(2):
                for k in range(KT):
                    last = t.matmul(ps[:, 3, q * KT + k:q * KT + k + 1], macc1[:, q, k * P:(k + 1) * P], ones[:, 0:1], start=True, stop=True)
            last.then_inc(s_modc, 1)
            pe.sem_inc(pe_slab, CREDIT_SLAB)

            def slab_product(slot, dst, k_ready=None):
                for k in range(KT):
                    if k_ready is not None:
                        pe.wait_ge(k_ready, k + 1)
                    for h in range(2):
                        cols_h = slice(h * H, (h + 1) * H)
                        last = three(dst[:, cols_h], w_hi[:, slot, k * P:(k + 1) * P], w_lo[:, slot, k * P:(k + 1) * P],
                                     A_hi[:, k, cols_h], A_lo[:, k, cols_h], k == 0, k == KT - 1)
                return last

            PS_FREE = {
                0: (dve_evac, 3, CREDIT_DVE_EVAC + 0), 1: (act_evac, 4, CREDIT_ACT_EVAC - 1), 2: (act_evac, 4, CREDIT_ACT_EVAC + 0),
                3: (dve_evac, 3, CREDIT_DVE_EVAC - 1), 4: (act_evac, 4, CREDIT_ACT_EVAC + 1), 5: (dve_evac, 3, CREDIT_DVE_EVAC + 1),
                6: (act_evac, 4, CREDIT_ACT_EVAC + 2)}
            with pe.Fori(0, KT) as ch:
                for kind in range(NK):
                    s, per, off = PS_FREE[kind]
                    pe.wait_ge(s, ch * per + off)
                    pe.wait_ge(w_lo_done, ch * NK + (kind + 1 + CREDIT_SLAB))
                    slab_product(W_SLOT[kind], ps[:, PS_SLOT[kind], :], s_hlo if kind == 0 else None).then_inc(pe_slab, 1)

            n0 = NK * KT

            def statistic(dst, src, ready, done):
                for k in range(KT):
                    pe.wait_ge(ready, k + 1)
                    for h in range(2):
                        last = t.matmul(dst[:, h * H:(h + 1) * H], mean_w[:], src(k, h), start=(k == 0), stop=(k == KT - 1))
                last.then_inc(done, 1)

            pe.wait_ge(act_evac, CREDIT_ACT_EVAC + 4 * KT)
            pe.wait_ge(dve_evac, CREDIT_DVE_EVAC + 3 * KT)
            for j in range(KT):
                slot, _, _ = slab_turn(n0 + j)
                pe.wait_ge(w_lo_done, n0 + j + 1 + CREDIT_SLAB)
                if j >= 2:
                    pe.wait_ge(s_ma, j - 1)
                slab_product(slot, ps[:, j % 2, :], s_alo if j == 0 else None).then_inc(pe_slab, 1)
                if j == 1:
                    statistic(ps[:, 2, :], lambda k, h: conf[:, k * S + h * H:k * S + (h + 1) * H], s_conf, s_mean)
                if j == 4:
                    statistic(ps[:, 3, :], lambda k, h: conf_sq[:, k, h * H:(h + 1) * H], s_sq, s_var)

            def rows_sum(q, slot):
                for h in range(2):
                    last = t.matmul(ps[:, slot, h * H:(h + 1) * H], ones[:], rows[:, q, h * H:(h + 1) * H], start=True, stop=True)
                last.then_inc(s_bc, 1)

            for j in range(KT):
                slot, _, _ = slab_turn(n0 + KT + j)
                pe.wait_ge(w_lo_done, n0 + KT + j + 1 + CREDIT_SLAB)
                if j < 2:
                    pe.wait_ge(s_ma, KT - 1 + j)
                else:
                    pe.wait_ge(ev2, j - 1)
                for k in range(KT):
                    if j == 0:
                        pe.wait_ge(s_blo, k + 1)
                    for h in range(2):
                        ch_ = slice(h * H, (h + 1) * H)
                        last = three(ps[:, j % 2, ch_], w_hi[:, slot, k * P:(k + 1) * P], w_lo[:, slot, k * P:(k + 1) * P],
                                     B_hi[:, k, ch_], B_lo[:, k, ch_], k == 0, k == KT - 1)
                last.then_inc(pe_slab, 1)
                if j == 1:
                    rows_sum(GT1, 2)
                    rows_sum(SH2, 3)
                if j == 3:
                    pe.wait_ge(s_bcev, 2)
                    rows_sum(A2, 2)
                    rows_sum(GT2, 3)

            def h2_transpose(i):
                pe.wait_ge(s_h2, i + 1)
                if i == 0:
                    pe.wait_ge(s_bcdv, 1)
                else:
                    pe.wait_ge(s_h2Tc, i)
                for k in range(KT):
                    last = t.transpose(ps[:, 2, k * P:(k + 1) * P], h2[:, i % 2, k * P:(k + 1) * P], ident[:])
                last.then_inc(s_h2T, 1)

            def router(i):
                pe.wait_ge(s_h2Tc, i + 1)
                pe.wait_ge(s_wr_in, 64)
                if i == 0:
                    pe.wait_ge(s_bcev, 3)
                else:
                    pe.wait_ge(s_lgev, i)
                for k in range(KT):
                    last = t.matmul(ps[:, 3, 0:NR], s2[:, k * P:(k + 1) * P], w_r[:, k, :], start=(k == 0), stop=(k == KT - 1))
                last.then_inc(s_lg, 1)

            pe.wait_ge(s_mlo, KT)
            for i in range(NT):
                pe.wait_ge(ev2, KT - 1 + i)
                for k in range(KT):
                    if i == 0:
                        pe.wait_ge(s_olo, k + 1)
                    for h in range(2):
                        ch_ = slice(h * H, (h + 1) * H)
                        last = three(ps[:, i % 2, ch_], A_hi[:, k, i * P:(i + 1) * P], A_lo[:, k, i * P:(i + 1) * P],
                                     B_hi[:, k, ch_], B_lo[:, k, ch_], k == 0, k == KT - 1)
                last.then_inc(pe_o, 1)
                if i >= 2:
                    router(i - 2)
                if i >= 1:
                    h2_transpose(i - 1)
            router(NT - 2)
            h2_transpose(NT - 1)
            router(NT - 1)
            pe.wait_ge(s_mask, 1)
            pe.wait_ge(ev2, KT + NT)
            t.matmul(ps[:, 0, 0:NT * NE], tri[:], mask[:].rearrange("p i e -> p (i e)"), start=True, stop=False)
            t.matmul(ps[:, 0, 0:NT * NE], ones[:], cum[:, 0:NT, :].rearrange("p i e -> p (i e)"), start=False, stop=True)
            t.matmul(ps[:, 0, H:H + NE], ones[:], cum[:, NT, :], start=True, stop=True).then_inc(s_rank, 1)

            for s, n in ((t_done, 1), (d_used, CREDIT_DOWN)):
                pe.sem_inc(s, n)
            pe.wait_ge(s_pos, 1)

            def rows_transpose(slot):
                for k in range(KT):
                    last = t.transpose(ps[:, 1, k * P:(k + 1) * P], xg[:, slot, k * P:(k + 1) * P], ident[:])
                last.then_inc(t_done, 1)

            def hidden_transpose(half):
                for f in range(2):
                    last = t.transpose(ps[:, 3, half * 4 * P + f * P:half * 4 * P + (f + 1) * P], hid[:, half, f * P:(f + 1) * P], ident[:])
                last.then_inc(ht_ps, 1)

            def gate_up(half, slot, b):
                dst = ps[:, 0, half * F:(half + 1) * F].rearrange("p (w n) -> p w n", w=2)
                for q in range(4):
                    if half == 0:
                        pe.wait_ge(gu_lo, b * 4 + (q + 1))
                    for kk in range(2):
                        k = 2 * q + kk

                        def part(buf):
                            return buf[:, q, kk * D:(kk + 1) * D].rearrange("p (w n) -> p w n", w=2)[:, :, half * F // 2:(half + 1) * F // 2]
                        last = three(dst, xT_hi[:, slot, k * P:(k + 1) * P], xT_lo[:, slot, k * P:(k + 1) * P],
                                     part(e_hi), part(e_lo), k == 0, k == KT - 1)
                    if half == 1:
                        last.then_inc(gu_used, 1)
                if half == 0:
                    last.then_inc(gu0, 1)

            def down(f):
                q, kk = f // 2, f % 2
                for h in range(2):
                    ch_ = slice(kk * D + h * H, kk * D + (h + 1) * H)
                    last = three(ps[:, 2, h * H:(h + 1) * H], hT_hi[:, f, :], hT_lo[:, f, :],
                                 e_hi[:, 4 + q, ch_], e_lo[:, 4 + q, ch_], f == 0, f == FT - 1)
                if kk == 1:
                    last.then_inc(d_used, 1)

            n_blk = pe.value_load(tab[0:1, NBLK:NBLK + 1], min_val=1, max_val=NBLK - 1)
            pe.wait_ge(xg_full[0], 16)
            rows_transpose(0)
            with pe.Fori(0, NBLK // 2) as pair:
                for s in range(2):
                    with pe.If(pair * 2 + s < n_blk):
                        b = pair * 2 + s
                        pe.wait_ge(xTlo, b + 1)
                        pe.wait_ge(hd0, b + 1)
                        gate_up(0, s, b)
                        pe.wait_ge(hd1, b + 1)
                        gate_up(1, s, b)
                        pe.wait_ge(hd0, b + 2)
                        pe.wait_ge(ht_lo, b * 2 + (CREDIT_DOWN - 1))
                        hidden_transpose(0)
                        pe.wait_ge(xg_full[1 - s], pair * 16 + 16 * (1 + s))
                        rows_transpose(1 - s)
                        pe.wait_ge(ht_lo, b * 2 + (1 + CREDIT_DOWN))
                        pe.wait_ge(d_lo, b * 2 + (1 + CREDIT_DOWN))
                        pe.wait_ge(y_ev, b + 1)
                        down(0)
                        pe.wait_ge(hd1, b + 2)
                        hidden_transpose(1)
                        down(1)
                        pe.wait_ge(ht_lo, b * 2 + (2 + CREDIT_DOWN))
                        pe.wait_ge(d_lo, b * 2 + (2 + CREDIT_DOWN))
                        down(2)
                        down(3)


_INS = ["x", "c", "w_ada", "b_ada", "g_norm1", "w_in", "conv_a", "w_a_out", "conv_b", "b_conv_b", "ln_conv_g", "ln_conv_b",
        "w_b_out", "w_o", "g_norm2", "w_router_g", "b_router_g", "w_router_e", "b_router_e", "w_gate", "w_up", "w_down", "g_final"]


def kernel(**inputs):
    import concourse.bacc as _bacc
    from concourse.bass_utils import run_bass_kernel_spmd as _run

    nc = _bacc.Bacc("TRN2", target_bir_lowering=False, num_devices=1)
    arrays, args = {}, []
    for name in _INS:
        a = np.ascontiguousarray(inputs[name])
        if name == "b_ada":
            a = a.reshape(6, -1)
        elif name == "g_final":
            a = a.reshape(1, -1)
        elif a.ndim >= 3 or name in ("w_ada", "w_in"):
            a = a.reshape(a.shape[1:])
        arrays[f"in_{name}_dram"] = a
        args.append(nc.dram_tensor(f"in_{name}_dram", a.shape, mybir.dt.from_np(a.dtype), kind="ExternalInput").ap())
    S, D = arrays["in_x_dram"].shape
    args.append(nc.dram_tensor("out_0_dram", (S, D), F32, kind="ExternalOutput").ap())
    encoder_block(nc, *args)
    r = _run(nc, [arrays], core_ids=[0])
    return r.results[0]["out_0_dram"].reshape(1, S, D)
```

```python
from contextlib import ExitStack

import numpy as np

import concourse.bass as bass
from concourse import mybir

F32 = mybir.dt.float32
F32R = mybir.dt.float32r
I32 = mybir.dt.int32
ALU = mybir.AluOpType
ACT = mybir.ActivationFunctionType
AX_X = mybir.AxisListType.X

P = 128
RMS_EPS = 1e-6
LN_EPS = 1e-5
NEG = -3.0e38

KINDS = ["conf_gate", "conf_value", "short_c", "short_x", "short_b", "gate_a", "gate_b"]
W_IN_GROUP = {"short_b": 0, "short_c": 1, "short_x": 2, "conf_value": 3, "conf_gate": 4, "gate_a": 5, "gate_b": 6}
NK = len(KINDS)
W_SLOT = [0, 1, 2, 0, 1, 2, 1]
W_TURN = [0, 0, 0, 1, 1, 1, 2]
W_BACK = [4, 2, 4, 3, 3, 3, 2]
W_PER_ROUND = [2, 3, 2]
PS_SLOT = [0, 1, 2, 3, 0, 1, 2]

ROW_CONV_A, ROW_BIAS_B, ROW_LN_G, ROW_LN_B, ROW_G1, ROW_SH, ROW_SC, ROW_C = 31, 34, 35, 36, 37, 38, 39, 40
N_ROWS = 41

CREDIT_SLAB = NK
CREDIT_ACT_EVAC = 4
CREDIT_DVE_EVAC = 3
CREDIT_FREE = 1
CREDIT_STORE = 2
CREDIT_DOWN = 2


def slab_turn(n):
    j = n - 8 * NK
    slot = j % 3
    before = [8 * NK - 4, 8 * NK - 1, 8 * NK - 2][j] if j < 3 else n - 3
    return slot, 8 * W_PER_ROUND[slot] + j // 3, before


def encoder_block(nc, x, c, w_ada, b_ada, g_norm1, w_in, conv_a, w_a_out, conv_b, b_conv_b, ln_g, ln_b,
                  w_b_out, w_o, g_norm2, w_rg, b_rg, w_re, b_re, w_gate, w_up, w_down, g_final, out):
    S, D = x.shape
    KT = D // P
    NT = S // P
    H = S // 2
    KB, KA = conv_b.shape[0], conv_a.shape[0]
    PAD_B, PAD_A = KB // 2, KA // 2
    NG = w_rg.shape[1]
    NE = w_re.shape[1]
    EPG = NE // NG
    F = w_gate.shape[2]
    FT = F // P
    PAIRS = 2 * S
    NBLK = PAIRS // P + NE
    NR = NG + NE
    assert D == S == 1024 and KT == 8 and NT == 8 and F == 512 and NBLK % 2 == 0

    with ExitStack() as ctx:
        base = (nc.sbuf_base + 63) // 64 * 64

        def at(name, offset, shape, dtype):
            return nc.alloc_sbuf_tensor_at(name, shape, dtype, offset=base + offset)

        T4 = 4 * D
        oA, oAl, oB, oBl = 0, 8 * T4, 16 * T4, 24 * T4
        oW = 32 * T4
        oS = oW + 9 * T4
        oR = oS + 4 * T4
        oM = oR + 4 * T4

        A_hi = at("A_hi", oA, [P, KT, S], F32R)
        A_lo = at("A_lo", oAl, [P, KT, S], F32R)
        B_hi = at("B_hi", oB, [P, KT, S], F32R)
        B_lo = at("B_lo", oBl, [P, KT, S], F32R)
        xn = at("xn", oB, [P, NT, D], F32)
        xnT = at("xnT", oAl, [P, KT, S], F32)
        conf = at("conf", oB, [P, KT * S], F32)
        conf_sq = at("conf_sq", oBl, [P, KT, S], F32)
        prow = at("prow", oBl, [P, D], F32)
        macc1 = at("macc1", oBl + T4, [P, 2, D], F32)
        hsc = at("hsc", oBl + 6 * T4, [P, 2, S], F32)
        junk0 = at("junk0", oBl + 5 * T4, [P, D], F32)
        sig_v = at("sig_v", oBl, [P, S], F32)
        c_sb = at("c_sb", oBl + T4, [P, S], F32)
        cx = at("cx", oBl + 2 * T4, [P, S + 2 * PAD_A], F32)
        conv_acc_a = at("conv_acc_a", oBl + 3 * T4 + 32, [P, S], F32)
        conv_acc_b = at("conv_acc_b", oBl + 4 * T4 + 32, [P, S], F32)
        gate_st = at("gate_st", oBl + 5 * T4 + 32, [P, 2, S], F32)
        w_raw = at("w_raw", oW, [P, 3, KT * P], F32)
        w_hi = at("w_hi", oW + 3 * T4, [P, 3, KT * P], F32R)
        w_lo = at("w_lo", oW + 6 * T4, [P, 3, KT * P], F32R)
        stream = at("stream", oS, [P, 4, D], F32)
        rows = at("rows", oR, [P, 4, D], F32)
        GT1, SH2, A2, GT2 = range(4)
        top = [oM]

        def small(name, shape, dtype=F32):
            n = int(np.prod(shape[1:])) * 4
            t = at(name, top[0], shape, dtype)
            top[0] += (n + 31) // 32 * 32
            return t

        glu_w = S + 2 * PAD_B
        glu = small("glu", [P, glu_w])
        s1 = at("s1", oM, [P, S], F32)
        s2 = small("s2", [P, S])
        ident = small("ident", [P, P])
        ones = small("ones", [P, P])
        mean_w = small("mean_w", [P, P])
        cols = small("cols", [P, KT, N_ROWS])
        colc = small("colc", [P, N_ROWS])
        modc = small("modc", [P, 2, KT])
        a1 = small("a1", [P, KT])
        sig_c = small("sig_c", [P, KT])
        ss = small("ss", [P, NT])
        rstd = small("rstd", [P, NT])
        msq, root, newt = small("msq", [P, NT]), small("root", [P, NT]), small("newton", [P, NT])
        assert base + top[0] <= nc.sbuf_usable_end, (base + top[0], nc.sbuf_usable_end)

        junk3 = at("junk3", oW, [P, D], F32)
        h2 = at("h2", oW + T4, [P, 2, D], F32)
        w_r = at("w_r", oW + 3 * T4, [P, KT, NR], F32)
        b_r = at("b_r", oW + 3 * T4 + 2048, [P, NR], F32)
        logits = at("logits", oW + 3 * T4 + 4096, [P, NT, NR], F32)
        tri = at("tri", oW + 3 * T4 + 8192, [P, P], F32)
        onesr = ones
        ro = [oW + 3 * T4 + 8192 + 512]

        def rt(name, shape, dtype=F32):
            n = int(np.prod(shape[1:])) * 4
            t = at(name, ro[0], shape, dtype)
            ro[0] += (n + 31) // 32 * 32
            assert ro[0] <= oS + T4
            return t

        iota_g = rt("iota_g", [P, NT, NG])
        iota_e = rt("iota_e", [P, NT, EPG])
        thr = rt("thr", [P, NT])
        blk_no = rt("blk_no", [P, NBLK])
        gsm = rt("gsm", [P, 8, NT])
        oh_g = rt("oh_g", [P, NT, NG])
        tg = rt("tg", [P, NT, NG])
        te = rt("te", [P, NT, EPG])
        le = rt("le", [P, NT, EPG])
        oh_k = rt("oh_k", [P, 2, NT, EPG])
        big = rt("big", [P, NT, NE])
        e_k = rt("e_k", [P, 2, NT, NE])
        mask = rt("mask", [P, NT, NE])
        cum = rt("cum", [P, NT + 1, NE])
        cnt_e = rt("cnt_e", [NE, 1])
        cmp_nb = rt("cmp_nb", [NE, NT])
        nb_e = rt("nb_e", [NE, 1])
        nb_b = rt("nb_b", [NE, P])
        tri_i = rt("tri_i", [P, P])
        pend_e = rt("pend_e", [NE, 1])
        cmp_b = rt("cmp_b", [NE, NBLK + 1])
        posf = rt("posf", [P, 2, NT])
        blk_i = rt("blk_i", [P, 2, NT], I32)
        blkf = rt("blkf", [P, 2, NT])
        rowf = rt("rowf", [P, 2, NT])
        tok1 = rt("tok1", [P, NT])
        inv_b = rt("inv_b", [P, 2, NT, 2, NBLK])
        oh_r = at("oh_r", oW, [P, 2, NT, P], F32)
        iota_r = rt("iota_r", [P, P])
        no_row = rt("no_row", [P, NBLK])

        tab = at("tab", oM, [1, 64], I32)
        posi = at("posi", oM + 256, [P, 2, NT], I32)
        w_tok = at("w_tok", oM + 768, [P, 2, NT], F32)
        idx_all = at("idx_all", oM + 1280, [P, NBLK + 2], I32)
        w_all = at("w_all", oM + 1536, [P, NBLK], F32)
        g_idx = at("g_idx", oM + 2560, [P, 2], I32)
        s_idx = at("s_idx", oM + 2592, [P, 2], I32)
        w_blk = at("w_blk", oM + 2624, [P, 2], F32)
        hT_hi = at("hT_hi", oM + 4224, [P, FT, P], F32R)
        hT_lo = at("hT_lo", oM + 4224 + 2048, [P, FT, P], F32R)

        NCH = 6
        C8 = 2 * D
        e_raw = at("e_raw", 0, [P, NCH, C8], F32)
        e_hi = at("e_hi", NCH * 4 * C8, [P, NCH, C8], F32R)
        e_lo = at("e_lo", 2 * NCH * 4 * C8, [P, NCH, C8], F32R)
        oX = 3 * NCH * 4 * C8
        xT_hi = at("xT_hi", oX, [P, 2, KT * P], F32R)
        xT_lo = at("xT_lo", oX + 2 * T4, [P, 2, KT * P], F32R)
        y_sb = at("y_sb", oX + 4 * T4, [P, 2, D], F32)
        xg = at("xg", oX + 6 * T4, [P, 2, D], F32)
        sg = at("sg", oX + 8 * T4, [P, 2, F // 2], F32)
        hid = at("hid", oX + 8 * T4 + 2048, [P, 2, F // 2], F32)
        assert oX + 8 * T4 + 4096 <= oR

        f_x = [at("f_x0", 4 * 4 * C8, [P, 4, D], F32), at("f_x1", (NCH + 4) * 4 * C8, [P, 4, D], F32)]
        f_o = at("f_o", (2 * NCH + 4) * 4 * C8, [P, 4, D], F32)
        f_junk = at("f_junk", oX + 4 * T4, [P, D], F32)

        ps = ctx.enter_context(nc.psum_tensor("ps", [P, 4, S], F32))

        def dram(name, shape, dtype=F32):
            return nc.dram_tensor(name, shape, dtype, kind="Internal").ap()

        d_a = dram("d_short", [D, S])
        d_g = [dram("d_gate_a", [D, S]), dram("d_gate_b", [D, S])]
        d_ma = dram("d_ma", [D, S])
        d_x1 = dram("d_x1", [S, D])
        d_h2 = dram("d_h2", [S, D])

        def sem(name):
            return ctx.enter_context(nc.semaphore(name))

        s_par, s_const, s_fill = sem("params_in"), sem("const_ready"), sem("const_steps")
        s_rows_in, s_g2_in, s_wr_in = sem("bias_rows_in"), sem("gfin_in"), sem("router_in")
        st_full = [sem(f"stream_full{i}") for i in range(4)]
        st_free = [sem(f"stream_free{i}") for i in range(4)]
        wr_full = [sem(f"w_raw_full{i}") for i in range(3)]
        w_hi_done, w_lo_done, pe_slab = sem("w_hi_done"), sem("w_lo_done"), sem("pe_slab")
        act_evac, dve_evac = sem("act_evac"), sem("dve_evac")
        dv = sem("dve_step")
        dvl = sem("dve_loop_step")
        s_parT, s_cols, s_sigc = sem("parT"), sem("cols_ready"), sem("sig_c_ready")
        s_ssq, s_rstd, s_xn, s_xT, s_xTev = sem("ssq"), sem("rstd_x"), sem("xn_ready"), sem("xT_ps"), sem("xnT_ready")
        s_macc, s_modc, s_h, s_hhi, s_hlo = sem("macc1_ready"), sem("modc_ps"), sem("h_f32"), sem("h_hi"), sem("h_lo")
        sp_a, sp_g = sem("short_spilled"), [sem("gate_a_spilled"), sem("gate_b_spilled")]
        s_ahi, s_alo = sem("short_hi"), sem("short_lo")
        s_conf, s_mean, s_cent, s_sq, s_var = sem("conf_ready"), sem("mean_ps"), sem("centred"), sem("squared"), sem("var_ps")
        s_ln, s_lsig, s_sw, s_bhi, s_blo = sem("ln_t"), sem("ln_sig"), sem("swish"), sem("conf_hi"), sem("conf_lo")
        ev2 = sem("evac_out")
        s_ma, sp_ma = sem("ma_ready"), sem("ma_spilled")
        s_m, s_mhi, s_mlo = sem("m_f32"), sem("m_hi"), sem("m_lo")
        s_bc, s_bcev, s_bcdv = sem("rows_ps"), sem("rows_act"), sem("rows_dve")
        s_ohi, s_olo = sem("wo_hi"), sem("wo_lo")
        pe_o, s_x1, s_ss3, s_h2 = sem("pe_o"), sem("x1_ready"), sem("ssq3"), sem("h2_ready")
        sp_x1, sp_h2, s_h2T, s_h2Tc, s_lg, s_lgev = (sem("x1_spilled"), sem("h2_spilled"), sem("h2T_ps"), sem("h2T_sb"),
                                                     sem("logits_ps"), sem("logits_sb"))
        s_exp, s_mask, s_rank, s_tab, s_pos = sem("exp_ready"), sem("mask_ready"), sem("rank_ps"), sem("tab_ready"), sem("pos_ready")
        s_e = sem("exp_in")
        s_nb, s_start, s_pend, s_cmp, s_tabp = sem("blocks_ready"), sem("starts_ps"), sem("ends_ps"), sem("ends_cmp"), sem("tab_ps")
        s_ohr, s_inv, s_w, s_yw = sem("one_hot_rows"), sem("inverse_ps"), sem("w_blk_ready"), sem("y_weighted")
        e_full = [sem(f"expert_full{i}") for i in range(NCH)]
        gu_hi, gu_lo, gu_used = sem("gu_hi"), sem("gu_lo"), sem("gu_used")
        d_hi, d_lo, d_used = sem("down_hi"), sem("down_lo"), sem("down_used")
        xg_full = [sem("xg_full0"), sem("xg_full1")]
        t_done, xThi, xTlo = sem("xT_done"), sem("xT_hi_done"), sem("xT_lo_done")
        gu0, sgd, hd0, hd1, a_h = sem("gu0_done"), sem("sg_done"), sem("hid0_done"), sem("hid1_done"), sem("hid_half")
        ht_ps, ht_hi, ht_lo = sem("hT_ps"), sem("hT_hi_done"), sem("hT_lo_done")
        y_ev, y_st, h2_free, p_step, p_copy, moe_done = sem("y_evac"), sem("y_stored"), sem("h2_free"), sem("pool_step"), sem("pool_copy"), sem("moe_done")
        f_ssq, f_out, f_st = sem("f_ssq"), sem("f_out"), [sem(f"f_stored{i}") for i in range(4)]
        a_free, g_free, y_free = sem("short_free"), [sem("gate_a_free"), sem("gate_b_free")], sem("y_free")
        dve_held = sem("dve_held")
        x_full = [sem(f"x_full{i}") for i in range(NT)]
        s_a1, s_hp = sem("modulation_columns"), sem("h_f32_odd")
        sp_step = sem("sync_step")
        s_msq, s_root = sem("mean_square"), sem("root")
        s_lnv, s_lnr = sem("ln_var"), sem("ln_root")

        block = ctx.enter_context(nc.Block())

        M_ADA1 = 0
        M_ADA2 = M_ADA1 + 2 * KT
        M_A = M_ADA2 + 4 * KT
        M_GA = M_A + KT
        M_GB = M_GA + KT
        M_G2 = M_GB + 2 * KT
        M_WO = M_G2 + 1
        M_XR = M_WO + KT

        def tile(m):
            return stream[:, m % 4, :]

        def load_tile(sp, m, src):
            if m >= 4:
                sp.wait_ge(st_free[m % 4], m // 4)
            sp.dma_start(tile(m), src).then_inc(st_full[m % 4], 16)

        def wait_tile(eng, m):
            eng.wait_ge(st_full[m % 4], 16 * (m // 4 + 1))

        def slab_in(kind, ch):
            col = W_IN_GROUP[kind] * D
            return w_in[:, bass.ds(ch * P + col, P)].rearrange("(k p) n -> p k n", p=P)

        def slab_out(n):
            j = n - NK * KT
            w = w_a_out if j < KT else w_b_out
            return w[:, j % KT * P:(j % KT + 1) * P].rearrange("(k p) n -> p k n", p=P)

        raw3 = w_raw[:].rearrange("p s (k n) -> p s k n", k=KT)

        @block.sync
        def _(sp):
            def held(s, value):
                sp.wait_ge(s, value)
                sp.sem_inc(sp_step, 1)

            for src, r, n in ((conv_b, 0, KB), (conv_a, ROW_CONV_A, KA), (b_conv_b, ROW_BIAS_B, 1), (ln_g, ROW_LN_G, 1),
                              (ln_b, ROW_LN_B, 1), (g_norm1, ROW_G1, 1), (b_ada[0:2], ROW_SH, 2), (c, ROW_C, 1)):
                sp.dma_start(prow[r:r + n, :], src).then_inc(s_par, 16)
            for i in range(NT):
                sp.dma_start(xn[:, i, :], x[i * P:(i + 1) * P, :]).then_inc(x_full[i], 16)
                for q in range(2):
                    load_tile(sp, M_ADA1 + 2 * i + q, w_ada[i * P:(i + 1) * P, q * D:(q + 1) * D])
            sp.wait_ge(s_const, 1)
            sp.dma_start(rows[0:1, :, :], b_ada[2:6].unsqueeze(0)).then_inc(s_rows_in, 16)

            sp.wait_ge(s_cols, 2)
            with sp.Fori(0, KT) as ch:
                for kind in range(NK):
                    s = W_SLOT[kind]
                    held(w_lo_done, ch * NK + (kind - W_BACK[kind] + 1 + CREDIT_SLAB))
                    sp.dma_start(raw3[:, s], slab_in(KINDS[kind], ch)).then_inc(wr_full[s], 16)
                    if kind in (0, 2, 4, 5):
                        q = (0, 2, 4, 5).index(kind)
                        held(st_free[q], ch + M_ADA2 // 4)
                        sp.dma_start(stream[:, q, :], w_ada[bass.ds(ch * P, P), (2 + q) * D:(3 + q) * D]).then_inc(st_full[q], 16)

            def load_slab(n):
                slot, _, before = slab_turn(n)
                sp.wait_ge(w_lo_done, before + 1 + CREDIT_SLAB)
                sp.dma_start(raw3[:, slot], slab_out(n)).then_inc(wr_full[slot], 16)

            n0 = NK * KT
            for n in range(n0, n0 + 3):
                load_slab(n)
            for k in range(KT):
                sp.wait_ge(sp_a, 16 * (k + 1))
                load_tile(sp, M_A + k, d_a[k * P:(k + 1) * P, :])
            for j in range(KT):
                sp.wait_ge(sp_g[0], 16 * (j + 1))
                load_tile(sp, M_GA + j, d_g[0][j * P:(j + 1) * P, :])
                load_slab(n0 + 3 + j)
            for j in range(KT):
                sp.wait_ge(sp_g[1], 16 * (j + 1))
                load_tile(sp, M_GB + 2 * j, d_g[1][j * P:(j + 1) * P, :])
                sp.wait_ge(sp_ma, 16 * (j + 1))
                load_tile(sp, M_GB + 2 * j + 1, d_ma[j * P:(j + 1) * P, :])
                if j < KT - 3:
                    load_slab(n0 + KT + 3 + j)
            load_tile(sp, M_G2, g_norm2.partition_broadcast(P).rearrange("p a n -> p (a n)"))
            for k in range(KT):
                load_tile(sp, M_WO + k, w_o[k * P:(k + 1) * P, :])
            for i in range(NT):
                load_tile(sp, M_XR + i, x[i * P:(i + 1) * P, :])
                if i == 0:
                    sp.wait_ge(pe_slab, n0 + 2 * KT + CREDIT_SLAB)
                    sp.dma_start(w_r[:, :, 0:NG], w_rg.rearrange("(k p) n -> p k n", p=P)).then_inc(s_wr_in, 16)
                    sp.dma_start(w_r[:, :, NG:NR], w_re.rearrange("(k p) n -> p k n", p=P)).then_inc(s_wr_in, 16)
                    sp.dma_start(b_r[:, 0:NG], b_rg.partition_broadcast(P).rearrange("p a n -> p (a n)")).then_inc(s_wr_in, 16)
                    sp.dma_start(b_r[:, NG:NR], b_re.partition_broadcast(P).rearrange("p a n -> p (a n)")).then_inc(s_wr_in, 16)

            def load_gu(q, e):
                for part, w in ((0, w_gate), (1, w_up)):
                    dst = e_raw[:, q, :].rearrange("p (k w n) -> p k w n", k=2, w=2)[:, :, part, :]
                    src = w[bass.ds(e, 1), 2 * q * P:2 * (q + 1) * P, :].rearrange("a (k p) n -> p (a k) n", p=P)
                    sp.dma_start(dst, src).then_inc(e_full[q], 16)

            def load_down(q, e):
                src = w_down[bass.ds(e, 1), 2 * q * P:2 * (q + 1) * P, :].rearrange("a (k p) n -> p (a k) n", p=P)
                sp.dma_start(e_raw[:, 4 + q, :].rearrange("p (k n) -> p k n", k=2), src).then_inc(e_full[4 + q], 16)

            sp.wait_ge(pe_o, NT)
            for q in range(4):
                load_gu(q, 0)
            for q in range(2):
                load_down(q, 0)
            sp.wait_ge(s_tab, 1)
            n_blk = sp.value_load(tab[0:1, NBLK:NBLK + 1], min_val=1, max_val=NBLK - 1)
            with sp.Fori(0, NBLK) as b:
                with sp.If(b < n_blk):
                    with sp.If(b + 1 < n_blk):
                        e_next = sp.value_load(tab[0:1, bass.ds(b + 1, 1)], min_val=0, max_val=NE - 1)
                        for q in range(4):
                            held(gu_lo, b * 4 + (q + 1))
                            load_gu(q, e_next)
                        for q in range(2):
                            held(d_lo, b * 2 + (q + 1 + CREDIT_DOWN))
                            load_down(q, e_next)
                    with sp.If(n_blk < b + 2):
                        for q in range(4):
                            sp.wait_ge(gu_lo, b * 4 + (q + 1))
                            sp.sem_inc(e_full[q], 32)

            sp.wait_ge(moe_done, 1)
            for i in range(NT):
                sp.dma_start(f_x[i // 4][:, i % 4, :], d_x1[i * P:(i + 1) * P, :]).then_inc(x_full[i], 16)
                if i == 0:
                    sp.dma_start(rows[:, SH2, :], g_final.partition_broadcast(P).rearrange("p a n -> p (a n)")).then_inc(s_g2_in, 16)
            for i in range(NT):
                sp.wait_ge(f_out, i + 1)
                sp.dma_start(out[i * P:(i + 1) * P, :], f_o[:, i % 4, :]).then_inc(f_st[i % 4], 16)
            for stored in f_st:
                sp.wait_ge(stored, 16 * NT // 4)

        @block.gpsimd
        def _(pool):
            g = nc.gpsimd
            steps = [0]

            def step(ins):
                steps[0] += 1
                ins.then_inc(s_fill, 1)
                pool.wait_ge(s_fill, steps[0])

            def held(s, value):
                pool.wait_ge(s, value)
                pool.sem_inc(p_step, 1)

            g.memset(ones[:], 1.0)
            g.memset(mean_w[:], 1.0 / D)
            step(g.memset(ident[:], 0.0))
            step(g.affine_select(out=ident[:], in_=ident[:], compare_op=ALU.not_equal, fill=1.0, base=0,
                                 pattern=[[-1, P]], channel_multiplier=1))
            g.memset(rows[:], 0.0).then_inc(s_const, 1)
            pool.wait_ge(s_const, 1)

            pool.wait_ge(s_a1, 1)
            for k in range(1, KT, 2):
                if k >= 3:
                    pool.wait_ge(s_hlo, k - 1)
                g.tensor_scalar(hsc[:, 1, :], xnT[:, k, :], a1[:, k:k + 1], modc[:, 0, k:k + 1], ALU.mult, ALU.add).then_inc(s_hp, 1)

            pool.wait_ge(s_cols, 2)
            with pool.Fori(0, KT) as ch:
                held(dve_evac, ch * 3 + (3 + CREDIT_DVE_EVAC))
                pool.dma_start(d_a[bass.ds(ch * P, P), :], conv_acc_a[:]).then_inc(sp_a, 16)
                for q in range(2):
                    held(act_evac, ch * 4 + (3 + q + CREDIT_ACT_EVAC))
                    pool.dma_start(d_g[q][bass.ds(ch * P, P), :], gate_st[:, q, :]).then_inc(sp_g[q], 16)
                for spilled, free in ((sp_a, a_free), (sp_g[0], g_free[0]), (sp_g[1], g_free[1])):
                    pool.wait_ge(spilled, ch * 16 + 16)
                    pool.sem_inc(free, 1)
            for j in range(KT):
                pool.wait_ge(s_ma, j + 1)
                pool.dma_start(d_ma[j * P:(j + 1) * P, :], tile(M_GA + j)).then_inc(sp_ma, 16)
                pool.wait_ge(sp_ma, 16 * (j + 1))
                pool.sem_inc(st_free[(M_GA + j) % 4], 1)

            pool.wait_ge(pe_slab, NK * KT + 2 * KT + CREDIT_SLAB)
            pool.wait_ge(w_lo_done, NK * KT + 2 * KT + CREDIT_SLAB)
            step(g.affine_select(out=tri[:], in_=ones[:], compare_op=ALU.is_gt, fill=0.0, base=0,
                                 pattern=[[1, P]], channel_multiplier=-1))
            g.iota(iota_g[:], pattern=[[0, NT], [1, NG]], base=0, channel_multiplier=0, allow_small_or_imprecise_dtypes=True)
            g.iota(iota_e[:], pattern=[[0, NT], [1, EPG]], base=0, channel_multiplier=0, allow_small_or_imprecise_dtypes=True)
            g.iota(thr[:], pattern=[[P, NT]], base=0, channel_multiplier=0, allow_small_or_imprecise_dtypes=True)
            step(g.affine_select(out=tri_i[:], in_=ones[:], compare_op=ALU.is_ge, fill=0.0, base=0,
                                 pattern=[[1, P]], channel_multiplier=-1))
            g.iota(iota_r[:], pattern=[[1, P]], base=0, channel_multiplier=0, allow_small_or_imprecise_dtypes=True)
            g.iota(tok1[:], pattern=[[P, NT]], base=1, channel_multiplier=1, allow_small_or_imprecise_dtypes=True)
            g.iota(blk_no[:], pattern=[[1, NBLK]], base=0, channel_multiplier=0, allow_small_or_imprecise_dtypes=True)
            step(g.memset(cum[:, 0, :], 0.0))
            pool.sem_inc(s_const, 1)

            for i in range(NT):
                pool.wait_ge(s_x1, i + 1)
                pool.dma_start(d_x1[i * P:(i + 1) * P, :], tile(M_XR + i)).then_inc(sp_x1, 16)
                pool.wait_ge(s_h2, i + 1)
                pool.dma_start(d_h2[i * P:(i + 1) * P, :], h2[:, i % 2, :]).then_inc(sp_h2, 16)
                pool.wait_ge(sp_x1, 16 * (i + 1))
                pool.sem_inc(st_free[(M_XR + i) % 4], 1)
                pool.wait_ge(sp_h2, 16 * (i + 1))
                pool.sem_inc(h2_free, 1)

            step(g.memset(xg[:], 0.0))
            step(g.memset(idx_all[:, NBLK:], 2 * PAIRS))
            pool.wait_ge(s_pos, 1)

            def gather(slot, blk, copies):
                g.tensor_copy(g_idx[:, slot:slot + 1], idx_all[:, bass.ds(blk, 1)]).then_inc(p_copy, 1)
                held(p_copy, copies)
                g.indirect_dma_start(xg[:, slot, :], None, d_h2, bass.IndirectOffsetOnAxis(ap=g_idx[:, slot:slot + 1], axis=0),
                                     bounds_check=S - 1, oob_is_err=False).then_inc(xg_full[slot], 16)

            n_blk = pool.value_load(tab[0:1, NBLK:NBLK + 1], min_val=1, max_val=NBLK - 1)
            gather(0, 0, 1)
            gather(1, 1, 2)
            with pool.Fori(0, NBLK // 2) as pair:
                for s in range(2):
                    with pool.If(pair * 2 + s < n_blk):
                        b = pair * 2 + s
                        held(t_done, b + 2)
                        gather(s, b + 2, b * 2 + 3)
                        g.tensor_copy(s_idx[:, s:s + 1], idx_all[:, bass.ds(b, 1)]).then_inc(p_copy, 1)
                        held(p_copy, b * 2 + 4)
                        g.tensor_copy(w_blk[:, s:s + 1], w_all[:, bass.ds(b, 1)]).then_inc(s_w, 1)
                        pool.wait_ge(y_ev, b + 2)
                        g.tensor_tensor(y_sb[:, s, :], y_sb[:, s, :], rows[:, GT2, :], ALU.mult).then_inc(s_yw, 1)
                        held(s_yw, b + 1)
                        g.indirect_dma_start(d_x1, bass.IndirectOffsetOnAxis(ap=s_idx[:, s:s + 1], axis=0), y_sb[:, s, :], None,
                                             bounds_check=S - 1, oob_is_err=False, compute_op=ALU.add).then_inc(y_st, 16)
                        pool.wait_ge(y_st, b * 16 + 16)
                        pool.sem_inc(y_free, 1)
            pool.sem_inc(moe_done, 1)

        @block.scalar
        def _(act):
            a = nc.scalar
            def take_root(stage, i):
                act.wait_ge(s_msq, stage * NT + i + 1)
                a.activation(root[:, i:i + 1], msq[:, i:i + 1], ACT.Sqrt).then_inc(s_root, 1)

            act.wait_ge(s_cols, 1)
            a.activation(sig_c[:], cols[:, :, ROW_C], ACT.Sigmoid).then_inc(s_sigc, 1)
            for i in range(NT):
                act.wait_ge(x_full[i], 16)
                a.activation(junk0[:], xn[:, i, :], ACT.Square, accum_out=ss[:, i:i + 1]).then_inc(s_ssq, 1)
                take_root(0, i)
                act.wait_ge(s_rstd, i + 1)
                a.activation(xn[:, i, :], xn[:, i, :], ACT.Copy, scale=rstd[:, i:i + 1]).then_inc(s_xn, 1)
            act.sem_inc(act_evac, CREDIT_ACT_EVAC)
            for q in range(2):
                act.sem_inc(g_free[q], CREDIT_FREE)
            def split(n, slot, full, before):
                act.wait_ge(wr_full[slot], full)
                act.wait_ge(pe_slab, before)
                a.copy(w_hi[:, slot, :], w_raw[:, slot, :]).then_inc(w_hi_done, 1)

            act.wait_ge(s_cols, 2)
            for kind in range(2):
                split(kind, W_SLOT[kind], 16, CREDIT_SLAB)
            act.wait_ge(s_a1, 1)
            for k in range(KT):
                a.activation(A_hi[:, k, :], xnT[:, k, :], ACT.Identity, scale=a1[:, k:k + 1], bias=modc[:, 0, k:k + 1]).then_inc(s_hhi, 1)
            with act.Fori(0, KT) as ch:
                for kind in range(NK):
                    name = KINDS[kind]
                    src = ps[:, PS_SLOT[kind], :]
                    n_done = ch * NK + (kind + 1 + CREDIT_SLAB)
                    if name == "conf_gate":
                        act.wait_ge(dve_evac, ch * 3 + (1 - 3 + CREDIT_DVE_EVAC))
                        act.wait_ge(pe_slab, n_done)
                        a.activation(sig_v[:], src, ACT.Sigmoid).then_inc(act_evac, 1)
                    if name == "short_c":
                        act.wait_ge(dve_evac, ch * 3 + (2 - 3 + CREDIT_DVE_EVAC))
                        act.wait_ge(pe_slab, n_done)
                        a.copy(c_sb[:], src).then_inc(act_evac, 1)
                    if name in ("gate_a", "gate_b"):
                        q = 0 if name == "gate_a" else 1
                        act.wait_ge(g_free[q], ch + CREDIT_FREE)
                        act.wait_ge(pe_slab, n_done)
                        a.activation(gate_st[:, q, :], src, ACT.Sigmoid).then_inc(act_evac, 1)
                    k2, over = (kind + 2) % NK, (kind + 2) // NK
                    s = W_SLOT[k2]
                    split(None, s, ch * (16 * W_PER_ROUND[s]) + 16 * (over * W_PER_ROUND[s] + W_TURN[k2] + 1),
                          ch * NK + (kind + 2 - W_BACK[k2] + 1 + CREDIT_SLAB))

            n0 = NK * KT
            for k in range(KT):
                wait_tile(act, M_A + k)
                act.wait_ge(pe_slab, n0 + CREDIT_SLAB)
                a.copy(A_hi[:, k, :], tile(M_A + k)).then_inc(s_ahi, 1)

            def split2(n):
                if n < n0 + 2 * KT:
                    slot, turn, before = slab_turn(n)
                    split(n, slot, 16 * (turn + 1), before + 1 + CREDIT_SLAB)

            def swish_in(k):
                act.wait_ge(s_ln, k + 1)
                if k >= 1:
                    act.wait_ge(s_sw, k)
                a.activation(s1[:], conf[:, k * S:(k + 1) * S], ACT.Sigmoid, scale=cols[:, k, ROW_LN_G:ROW_LN_G + 1],
                             bias=cols[:, k, ROW_LN_B:ROW_LN_B + 1]).then_inc(s_lsig, 1)

            def conf_hi(k):
                act.wait_ge(s_sw, k + 1)
                a.copy(B_hi[:, k, :], s2[:]).then_inc(s_bhi, 1)

            for j in range(KT):
                split2(n0 + j + 2)
                if j == 1:
                    for spilled in (sp_a, sp_g[0], sp_g[1]):
                        act.wait_ge(spilled, 16 * KT)
                    for k in range(KT):
                        act.wait_ge(s_cent, k + 1)
                        a.activation(conf_sq[:, k, :], conf[:, k * S:(k + 1) * S], ACT.Square).then_inc(s_sq, 1)
                if j == 4:
                    act.wait_ge(s_lnv, 1)
                    a.activation(s1[:], ps[:, 3, :], ACT.Sqrt).then_inc(s_lnr, 1)
                for k in {4: [0, 1], 5: [2, 3], 6: [4, 5], 7: [6, 7]}.get(j, []):
                    swish_in(k)
                    conf_hi(k)
            for j in range(KT):
                act.wait_ge(s_m, j + 1)
                a.copy(A_hi[:, j, :], s2[:]).then_inc(s_mhi, 1)
                split2(n0 + KT + j + 2)
                if j == 1:
                    for q, slot in ((GT1, 2), (SH2, 3)):
                        act.wait_ge(s_bc, q + 1)
                        a.copy(rows[:, q, :], ps[:, slot, :]).then_inc(s_bcev, 1)
                if j == 3:
                    act.wait_ge(s_bc, 4)
                    a.copy(rows[:, GT2, :], ps[:, 3, :]).then_inc(s_bcev, 1)
            for k in range(KT):
                wait_tile(act, M_WO + k)
                act.wait_ge(pe_slab, n0 + 2 * KT + CREDIT_SLAB)
                a.copy(B_hi[:, k, :], tile(M_WO + k)).then_inc(s_ohi, 1)

            def h2_copy(i):
                act.wait_ge(s_h2T, i + 1)
                if i >= 1:
                    act.wait_ge(s_lg, i)
                a.copy(s2[:], ps[:, 2, :]).then_inc(s_h2Tc, 1)

            for i in range(NT):
                act.wait_ge(s_x1, i + 1)
                a.activation(junk3[:], tile(M_XR + i), ACT.Square, accum_out=ss[:, i:i + 1]).then_inc(s_ss3, 1)
                take_root(1, i)
                if i >= 1:
                    h2_copy(i - 1)
            h2_copy(NT - 1)
            act.wait_ge(s_e, 1)
            a.activation(tg[:], tg[:], ACT.Exp).then_inc(s_exp, 1)
            act.wait_ge(s_e, 2)
            a.activation(gsm[:, 5, :], gsm[:, 4, :], ACT.Exp).then_inc(s_exp, 1)

            act.sem_inc(y_ev, 1)
            act.sem_inc(y_free, CREDIT_STORE)

            def gu_split(q, full, before):
                act.wait_ge(e_full[q], full)
                if before is not None:
                    act.wait_ge(gu_used, before)
                a.copy(e_hi[:, q, :], e_raw[:, q, :]).then_inc(gu_hi, 1)

            for q in range(4):
                gu_split(q, 32, None)
            act.wait_ge(s_tab, 1)

            def x_hi(slot, value):
                act.wait_ge(t_done, value)
                a.copy(xT_hi[:, slot, :], ps[:, 1, :]).then_inc(xThi, 1)

            n_blk = act.value_load(tab[0:1, NBLK:NBLK + 1], min_val=1, max_val=NBLK - 1)
            x_hi(0, 2)
            with act.Fori(0, NBLK // 2) as pair:
                for s in range(2):
                    with act.If(pair * 2 + s < n_blk):
                        b = pair * 2 + s
                        for q in range(2):
                            act.wait_ge(e_full[4 + q], b * 16 + 16)
                            act.wait_ge(d_used, b * 2 + (q - 1 + CREDIT_DOWN))
                            a.copy(e_hi[:, 4 + q, :], e_raw[:, 4 + q, :]).then_inc(d_hi, 1)
                        act.wait_ge(gu0, b + 1)
                        a.activation(sg[:, 0, :], ps[:, 0, 0:F // 2], ACT.Sigmoid).then_inc(sgd, 1)
                        gu_split(0, b * 32 + 64, b * 4 + 1)
                        act.wait_ge(ht_ps, b * 2 + 1)
                        a.copy(hT_hi[:, 0:2, :], ps[:, 3, 0:2 * P]).then_inc(ht_hi, 1)
                        act.wait_ge(gu_used, b * 4 + 4)
                        a.activation(sg[:, 1, :], ps[:, 0, F:F + F // 2], ACT.Sigmoid).then_inc(sgd, 1)
                        gu_split(1, b * 32 + 64, b * 4 + 2)
                        act.wait_ge(ht_ps, b * 2 + 2)
                        a.copy(hT_hi[:, 2:4, :], ps[:, 3, 4 * P:6 * P]).then_inc(ht_hi, 1)
                        gu_split(2, b * 32 + 64, b * 4 + 3)
                        x_hi(1 - s, b + 3)
                        gu_split(3, b * 32 + 64, b * 4 + 4)
                        act.wait_ge(d_used, b * 2 + (2 + CREDIT_DOWN))
                        act.wait_ge(y_free, b + (CREDIT_STORE - 1))
                        act.wait_ge(s_w, b + 1)
                        a.activation(y_sb[:, s, :], ps[:, 2, :], ACT.Copy, scale=w_blk[:, s:s + 1]).then_inc(y_ev, 1)

            for i in range(NT):
                act.wait_ge(x_full[i], 32)
                a.activation(f_junk[:], f_x[i // 4][:, i % 4, :], ACT.Square, accum_out=ss[:, i:i + 1]).then_inc(f_ssq, 1)
                take_root(2, i)

        @block.vector
        def _(dve):
            v = nc.vector
            steps = [0]

            def step(ins):
                steps[0] += 1
                ins.then_inc(dv, 1)
                dve.wait_ge(dv, steps[0])

            def held(s, value):
                dve.wait_ge(s, value)
                dve.sem_inc(dve_held, 1)

            dve.wait_ge(s_parT, 1)
            v.tensor_copy(cols[:], ps[:, 2, 0:KT * N_ROWS]).then_inc(s_cols, 1)
            dve.wait_ge(s_cols, 1)
            dve.wait_ge(s_sigc, 1)
            step(v.tensor_tensor(cols[:, :, ROW_C], cols[:, :, ROW_C], sig_c[:], ALU.mult))
            dve.sem_inc(dve_evac, CREDIT_DVE_EVAC)
            dve.sem_inc(w_lo_done, CREDIT_SLAB)
            dve.sem_inc(a_free, CREDIT_FREE)
            dve.sem_inc(s_cols, 1)

            def split(slot, n_hi):
                dve.wait_ge(w_hi_done, n_hi)
                v.tensor_tensor(w_lo[:, slot, :], w_raw[:, slot, :], w_hi[:, slot, :].bitcast(F32), ALU.subtract).then_inc(w_lo_done, 1)


            def rms(stage, i):
                n = stage * NT + i + 1
                m, r, t = msq[:, i:i + 1], rstd[:, i:i + 1], newt[:, i:i + 1]
                v.tensor_scalar(m, ss[:, i:i + 1], 1.0 / D, RMS_EPS, ALU.mult, ALU.add).then_inc(s_msq, 1)
                dve.wait_ge(s_msq, n)
                dve.wait_ge(s_root, n)
                step(v.reciprocal(r, root[:, i:i + 1]))
                step(v.scalar_tensor_tensor(t, r, m, r, ALU.mult, ALU.mult))
                step(v.tensor_scalar(t, t, -0.5, 1.5, ALU.mult, ALU.add))
                return v.tensor_tensor(r, r, t, ALU.mult)

            def xT_evac(i):
                dve.wait_ge(s_xT, i + 1)
                v.tensor_copy(xnT[:, :, i * P:(i + 1) * P], ps[:, i % 2, :].rearrange("p (k n) -> p k n", k=KT)).then_inc(s_xTev, 1)

            for i in range(NT):
                dve.wait_ge(s_ssq, i + 1)
                rms(0, i).then_inc(s_rstd, 1)
                if i >= 1:
                    xT_evac(i - 1)
                for q in range(2):
                    m = M_ADA1 + 2 * i + q
                    wait_tile(dve, m)
                    if i == 0:
                        ins = v.tensor_scalar(macc1[:, q, :], tile(m), cols[:, i, ROW_C:ROW_C + 1], None, ALU.mult)
                    else:
                        ins = v.scalar_tensor_tensor(macc1[:, q, :], tile(m), cols[:, i, ROW_C:ROW_C + 1], macc1[:, q, :],
                                                     ALU.mult, ALU.add)
                    step(ins)
                    dve.sem_inc(st_free[m % 4], 1)
            dve.sem_inc(s_macc, 1)
            xT_evac(NT - 1)
            for kind in range(2):
                split(W_SLOT[kind], kind + 1)
            dve.wait_ge(s_modc, 1)
            step(v.tensor_tensor(modc[:], ps[:, 3, 0:2 * KT].rearrange("p (q k) -> p q k", q=2),
                                 cols[:, :, ROW_SH:ROW_SC + 1].rearrange("p k q -> p q k"), ALU.add))
            step(v.scalar_tensor_tensor(a1[:], modc[:, 1, :], 1.0, cols[:, :, ROW_G1], ALU.add, ALU.mult))
            dve.sem_inc(s_a1, 1)
            v.memset(glu[:, 0:PAD_B], 0.0)
            v.memset(glu[:, PAD_B + S:], 0.0)
            v.memset(cx[:, 0:PAD_A], 0.0)
            step(v.memset(cx[:, PAD_A + S:], 0.0))
            dve.wait_ge(s_xTev, NT)
            def h_even(k):
                if k >= 2:
                    dve.wait_ge(s_hlo, k - 1)
                v.tensor_scalar(hsc[:, 0, :], xnT[:, k, :], a1[:, k:k + 1], modc[:, 0, k:k + 1], ALU.mult, ALU.add).then_inc(s_h, 1)

            h_even(0)
            for k in range(KT):
                if k % 2 == 0:
                    dve.wait_ge(s_h, k // 2 + 1)
                else:
                    dve.wait_ge(s_hp, k // 2 + 1)
                dve.wait_ge(s_hhi, k + 1)
                v.tensor_tensor(A_lo[:, k, :], hsc[:, k % 2, :], A_hi[:, k, :].bitcast(F32), ALU.subtract).then_inc(s_hlo, 1)
                if k % 2 == 0 and k + 2 < KT:
                    h_even(k + 2)
            dve.wait_ge(s_rows_in, 16)

            TAPS = {1: range(0, 5), 2: range(5, 11), 3: range(11, 15), 4: range(15, 21), 5: range(21, 26), 6: range(26, KB)}
            N_STEPS = 1 + 4 + KB - 1 + KA
            with dve.Fori(0, KT) as ch:
                count = [0]

                def lstep(ins):
                    count[0] += 1
                    ins.then_inc(dvl, 1)
                    dve.wait_ge(dvl, ch * N_STEPS + count[0])

                for kind in range(NK):
                    name = KINDS[kind]
                    src = ps[:, PS_SLOT[kind], :]
                    n_done = ch * NK + (kind + 1 + CREDIT_SLAB)
                    if kind == 0:
                        lstep(v.tensor_copy(colc[:], cols[:, bass.ds(ch, 1), :].rearrange("p a n -> p (a n)")))
                    if name == "conf_value":
                        dve.wait_ge(act_evac, ch * 4 + (1 + CREDIT_ACT_EVAC))
                        dve.wait_ge(pe_slab, n_done)
                        v.tensor_tensor(glu[:, PAD_B:PAD_B + S], src, sig_v[:], ALU.mult).then_inc(dve_evac, 1)
                        dve.wait_ge(dve_evac, ch * 3 + (1 + CREDIT_DVE_EVAC))
                    if name == "short_x":
                        dve.wait_ge(act_evac, ch * 4 + (2 + CREDIT_ACT_EVAC))
                        dve.wait_ge(pe_slab, n_done)
                        v.tensor_tensor(cx[:, PAD_A:PAD_A + S], src, c_sb[:], ALU.mult).then_inc(dve_evac, 1)
                        dve.wait_ge(dve_evac, ch * 3 + (2 + CREDIT_DVE_EVAC))
                        dve.wait_ge(a_free, ch + CREDIT_FREE)
                        for t in range(KA):
                            w = colc[:, ROW_CONV_A + t:ROW_CONV_A + t + 1]
                            if t == 0:
                                lstep(v.tensor_scalar(conv_acc_a[:], cx[:, t:t + S], w, None, ALU.mult))
                            else:
                                lstep(v.scalar_tensor_tensor(conv_acc_a[:], cx[:, t:t + S], w, conv_acc_a[:], ALU.mult, ALU.add))
                    if name == "short_b":
                        dve.wait_ge(pe_slab, n_done)
                        v.tensor_tensor(conv_acc_a[:], src, conv_acc_a[:], ALU.mult).then_inc(dve_evac, 1)
                    k2 = (kind + 2) % NK
                    split(W_SLOT[k2], ch * NK + (kind + 3))
                    if kind in (0, 2, 4, 6):
                        q = kind // 2
                        dve.wait_ge(st_full[q], ch * 16 + 16 * (M_ADA2 // 4 + 1))
                        lstep(v.scalar_tensor_tensor(rows[:, q, :], stream[:, q, :], colc[:, ROW_C:ROW_C + 1], rows[:, q, :],
                                                     ALU.mult, ALU.add))
                        dve.sem_inc(st_free[q], 1)
                    for t in TAPS.get(kind, []):
                        w = colc[:, t:t + 1]
                        if t == 0:
                            lstep(v.tensor_scalar(conv_acc_b[:], glu[:, t:t + S], w, colc[:, ROW_BIAS_B:ROW_BIAS_B + 1], ALU.mult, ALU.add))
                        elif t < KB - 1:
                            lstep(v.scalar_tensor_tensor(conv_acc_b[:], glu[:, t:t + S], w, conv_acc_b[:], ALU.mult, ALU.add))
                        else:
                            v.scalar_tensor_tensor(conf[:, bass.ds(ch * S, S)], glu[:, t:t + S], w, conv_acc_b[:],
                                                   ALU.mult, ALU.add).then_inc(s_conf, 1)
                            held(s_conf, ch + 1)
                assert count[0] == N_STEPS, count

            n0 = NK * KT
            for k in range(KT):
                dve.wait_ge(s_ahi, k + 1)
                v.tensor_tensor(A_lo[:, k, :], tile(M_A + k), A_hi[:, k, :].bitcast(F32), ALU.subtract).then_inc(s_alo, 1)
                dve.wait_ge(s_alo, k + 1)
                dve.sem_inc(st_free[(M_A + k) % 4], 1)

            def split2(n):
                if n < n0 + 2 * KT:
                    split(slab_turn(n)[0], n + 1)

            def ln_t(k):
                u = conf[:, k * S:(k + 1) * S]
                v.tensor_tensor(u, ps[:, 3, :], u, ALU.mult).then_inc(s_ln, 1)

            def swish(k):
                u = conf[:, k * S:(k + 1) * S]
                dve.wait_ge(s_lsig, k + 1)
                step(v.tensor_scalar(u, u, cols[:, k, ROW_LN_G:ROW_LN_G + 1], cols[:, k, ROW_LN_B:ROW_LN_B + 1], ALU.mult, ALU.add))
                if k >= 1:
                    dve.wait_ge(s_blo, k)
                v.tensor_tensor(s2[:], u, s1[:], ALU.mult).then_inc(s_sw, 1)
                if k + 1 < KT:
                    ln_t(k + 1)
                dve.wait_ge(s_bhi, k + 1)
                v.tensor_tensor(B_lo[:, k, :], s2[:], B_hi[:, k, :].bitcast(F32), ALU.subtract).then_inc(s_blo, 1)

            for j in range(KT):
                dve.wait_ge(pe_slab, n0 + j + 1 + CREDIT_SLAB)
                wait_tile(dve, M_GA + j)
                v.tensor_tensor(tile(M_GA + j), ps[:, j % 2, :], tile(M_GA + j), ALU.mult).then_inc(s_ma, 1)
                split2(n0 + j + 2)
                if j == 1:
                    dve.wait_ge(s_mean, 1)
                    for k in range(KT):
                        u = conf[:, k * S:(k + 1) * S]
                        v.scalar_tensor_tensor(u, ps[:, 2, :], -1.0, u, ALU.mult, ALU.add).then_inc(s_cent, 1)
                if j == 4:
                    dve.wait_ge(s_cent, KT)
                    dve.wait_ge(s_var, 1)
                    v.tensor_scalar(ps[:, 3, :], ps[:, 3, :], LN_EPS, None, ALU.add).then_inc(s_lnv, 1)
                    dve.wait_ge(s_lnv, 1)
                    dve.wait_ge(s_lnr, 1)
                    step(v.reciprocal(s1[:], s1[:]))
                    step(v.tensor_tensor(s2[:], s1[:], s1[:], ALU.mult))
                    step(v.tensor_tensor(s2[:], s2[:], ps[:, 3, :], ALU.mult))
                    step(v.tensor_scalar(s2[:], s2[:], -0.5, 1.5, ALU.mult, ALU.add))
                    step(v.tensor_tensor(ps[:, 3, :], s1[:], s2[:], ALU.mult))
                    ln_t(0)
                for k in {4: [0, 1], 5: [2, 3], 6: [4, 5], 7: [6, 7]}.get(j, []):
                    swish(k)
            for j in range(KT):
                mg, mm = M_GB + 2 * j, M_GB + 2 * j + 1
                dve.wait_ge(pe_slab, n0 + KT + j + 1 + CREDIT_SLAB)
                wait_tile(dve, mg)
                step(v.tensor_tensor(s1[:], ps[:, j % 2, :], tile(mg), ALU.mult))
                dve.sem_inc(ev2, 1)
                dve.sem_inc(st_free[mg % 4], 1)
                wait_tile(dve, mm)
                if j >= 1:
                    dve.wait_ge(s_mlo, j)
                else:
                    dve.wait_ge(s_blo, KT)
                v.tensor_tensor(s2[:], s1[:], tile(mm), ALU.add).then_inc(s_m, 1)
                dve.wait_ge(s_m, j + 1)
                dve.sem_inc(st_free[mm % 4], 1)
                dve.wait_ge(s_mhi, j + 1)
                v.tensor_tensor(A_lo[:, j, :], s2[:], A_hi[:, j, :].bitcast(F32), ALU.subtract).then_inc(s_mlo, 1)
                split2(n0 + KT + j + 2)
                if j == 3:
                    dve.wait_ge(s_bc, A2 + 1)
                    step(v.tensor_copy(rows[:, A2, :], ps[:, 2, :]))
                    dve.sem_inc(s_bcdv, 1)
            wait_tile(dve, M_G2)
            step(v.scalar_tensor_tensor(rows[:, A2, :], rows[:, A2, :], 1.0, tile(M_G2), ALU.add, ALU.mult))
            dve.sem_inc(st_free[M_G2 % 4], 1)
            for k in range(KT):
                dve.wait_ge(s_ohi, k + 1)
                v.tensor_tensor(B_lo[:, k, :], tile(M_WO + k), B_hi[:, k, :].bitcast(F32), ALU.subtract).then_inc(s_olo, 1)
                dve.wait_ge(s_olo, k + 1)
                dve.sem_inc(st_free[(M_WO + k) % 4], 1)
            dve.wait_ge(s_bcev, 3)

            def logits_evac(i):
                dve.wait_ge(s_lg, i + 1)
                dve.wait_ge(s_wr_in, 64)
                v.tensor_tensor(logits[:, i, :], ps[:, 3, 0:NR], b_r[:], ALU.add).then_inc(s_lgev, 1)

            for i in range(NT):
                xt = tile(M_XR + i)
                dve.wait_ge(pe_o, i + 1)
                step(v.tensor_tensor(s1[:], ps[:, i % 2, :], rows[:, GT1, :], ALU.mult))
                dve.sem_inc(ev2, 1)
                wait_tile(dve, M_XR + i)
                v.tensor_tensor(xt, s1[:], xt, ALU.add).then_inc(s_x1, 1)
                if i >= 2:
                    logits_evac(i - 2)
                dve.wait_ge(s_ss3, i + 1)
                step(rms(1, i))
                if i >= 2:
                    dve.wait_ge(h2_free, i - 1)
                    dve.wait_ge(s_h2T, i - 1)
                hh = h2[:, i % 2, :]
                step(v.scalar_tensor_tensor(hh, xt, rstd[:, i:i + 1], rows[:, A2, :], ALU.mult, ALU.mult))
                v.tensor_tensor(hh, hh, rows[:, SH2, :], ALU.add).then_inc(s_h2, 1)
            logits_evac(NT - 2)
            logits_evac(NT - 1)
            dve.wait_ge(s_lgev, NT)
            dve.wait_ge(s_const, 2)

            def bc(ap, shape):
                return ap.to_broadcast(shape)

            FAR = 1.0e3

            def row(r):
                return gsm[:, r, :]

            def one_hot(dst, values, best, iota, width, tmp):
                shape = [P, NT, width]
                step(v.tensor_tensor(tmp, values, bc(best.unsqueeze(2), shape), ALU.is_equal))
                step(v.scalar_tensor_tensor(tmp, tmp, -FAR, iota, ALU.mult, ALU.add))
                step(v.tensor_reduce(row(2), tmp, AX_X, ALU.min))
                step(v.tensor_tensor(dst, tmp, bc(row(2).unsqueeze(2), shape), ALU.is_equal))

            lg, lexp = logits[:, :, 0:NG], logits[:, :, NG:NR]
            step(v.tensor_reduce(row(0), lg, AX_X, ALU.max))
            step(v.tensor_tensor(tg[:], lg, bc(row(0).unsqueeze(2), [P, NT, NG]), ALU.subtract))
            dve.sem_inc(s_e, 1)
            dve.wait_ge(s_exp, 1)
            step(v.tensor_reduce(row(1), tg[:], AX_X, ALU.add))
            step(v.reciprocal(row(1), row(1)))
            one_hot(oh_g[:], lg, row(0), iota_g[:], NG, tg[:])
            b4 = big[:].rearrange("p i (g e) -> p i g e", g=NG)
            step(v.tensor_tensor(b4, lexp.rearrange("p i (g e) -> p i g e", g=NG), bc(oh_g[:].unsqueeze(3), [P, NT, NG, EPG]), ALU.mult))
            step(v.tensor_reduce(le[:], big[:].rearrange("p i (g e) -> p i e g", g=NG), AX_X, ALU.add))
            step(v.tensor_reduce(row(3), le[:], AX_X, ALU.max))
            one_hot(oh_k[:, 0], le[:], row(3), iota_e[:], EPG, te[:])
            step(v.scalar_tensor_tensor(le[:], oh_k[:, 0], NEG, le[:], ALU.mult, ALU.add))
            step(v.tensor_reduce(row(4), le[:], AX_X, ALU.max))
            one_hot(oh_k[:, 1], le[:], row(4), iota_e[:], EPG, te[:])
            step(v.tensor_tensor(row(4), row(4), row(3), ALU.subtract))
            dve.sem_inc(s_e, 1)
            for k in range(2):
                e4 = e_k[:, k].rearrange("p i (g e) -> p i g e", g=NG)
                step(v.tensor_tensor(e4, bc(oh_g[:].unsqueeze(3), [P, NT, NG, EPG]), bc(oh_k[:, k].unsqueeze(2), [P, NT, NG, EPG]), ALU.mult))
            step(v.tensor_tensor(mask[:], e_k[:, 0], e_k[:, 1], ALU.add))
            for i in range(NT):
                step(v.tensor_tensor(cum[:, i + 1, :], cum[:, i, :], mask[:, i, :], ALU.add))
            dve.sem_inc(s_mask, 1)
            dve.wait_ge(s_exp, 2)
            step(v.tensor_scalar(row(6), row(5), 1.0, None, ALU.add))
            step(v.reciprocal(row(6), row(6)))
            step(v.tensor_tensor(w_tok[:, 0, :], row(6), row(1), ALU.mult))
            step(v.tensor_tensor(w_tok[:, 1, :], w_tok[:, 0, :], row(5), ALU.mult))
            dve.wait_ge(s_rank, 1)
            step(v.tensor_tensor(cnt_e[:], ps[0:NE, 1, 0:1], ident[0:NE, 0:1], ALU.max))
            step(v.tensor_scalar(cmp_nb[:], thr[0:NE, :], cnt_e[:, 0:1], None, ALU.is_lt))
            step(v.tensor_reduce(nb_e[:], cmp_nb[:], AX_X, ALU.add))
            step(v.tensor_scalar(nb_b[:], ones[0:NE, :], nb_e[:, 0:1], None, ALU.mult))
            dve.sem_inc(s_nb, 1)
            dve.wait_ge(s_start, 1)
            step(v.tensor_copy(cum[:, 0, :], ps[:, 3, 0:NE]))
            step(v.scalar_tensor_tensor(mask[:], bc(cum[:, 0, :].unsqueeze(1), [P, NT, NE]), float(P),
                                        ps[:, 0, 0:NT * NE].rearrange("p (i e) -> p i e", i=NT), ALU.mult, ALU.add))
            for k in range(2):
                step(v.tensor_tensor(e_k[:, k], e_k[:, k], mask[:], ALU.mult))
                step(v.tensor_reduce(posf[:, k, :], e_k[:, k], AX_X, ALU.add))
            step(v.tensor_copy(posi[:], posf[:]))
            dve.wait_ge(h2_free, NT)
            step(v.tensor_scalar(blk_i[:], posi[:], P.bit_length() - 1, None, ALU.arith_shift_right))
            step(v.tensor_copy(blkf[:], blk_i[:]))
            step(v.scalar_tensor_tensor(rowf[:], blkf[:], -float(P), posf[:], ALU.mult, ALU.add))
            for k in range(2):
                step(v.tensor_tensor(inv_b[:, k, :, 1, :], bc(blk_no[:].unsqueeze(1), [P, NT, NBLK]),
                                     bc(blkf[:, k, :].unsqueeze(2), [P, NT, NBLK]), ALU.is_equal))
                step(v.tensor_tensor(inv_b[:, k, :, 0, :], inv_b[:, k, :, 1, :], bc(tok1[:].unsqueeze(2), [P, NT, NBLK]), ALU.mult))
                step(v.tensor_tensor(inv_b[:, k, :, 1, :], inv_b[:, k, :, 1, :], bc(w_tok[:, k, :].unsqueeze(2), [P, NT, NBLK]), ALU.mult))
                v.tensor_tensor(oh_r[:, k], bc(iota_r[:].unsqueeze(1), [P, NT, P]), bc(rowf[:, k, :].unsqueeze(2), [P, NT, P]),
                                ALU.is_equal).then_inc(s_ohr, 1)
                if k == 0:
                    dve.wait_ge(s_pend, 1)
                    step(v.tensor_copy(pend_e[:], ps[0:NE, 3, H:H + 1]))
                    step(v.tensor_scalar(cmp_b[:, 0:NBLK], blk_no[0:NE, :], pend_e[:, 0:1], None, ALU.is_ge))
                    step(v.tensor_copy(cmp_b[:, NBLK:NBLK + 1], nb_e[:]))
                    dve.sem_inc(s_cmp, 1)
            dve.wait_ge(s_tabp, 1)
            step(v.tensor_copy(tab[:, NBLK:NBLK + 1], ps[0:1, 1, H + NBLK:H + NBLK + 1]))
            v.tensor_scalar(tab[:, 0:NBLK], ps[0:1, 1, H:H + NBLK], float(NE - 1), None, ALU.min).then_inc(s_tab, 1)
            dve.wait_ge(s_inv, 1)
            step(v.tensor_scalar(no_row[:], ps[:, 2, 0:NBLK], 0.0, 2.0 * PAIRS, ALU.is_equal, ALU.mult))
            step(v.scalar_tensor_tensor(idx_all[:, 0:NBLK], ps[:, 2, 0:NBLK], -1.0, no_row[:], ALU.add, ALU.add))
            v.tensor_copy(w_all[:], ps[:, 2, NBLK:2 * NBLK]).then_inc(s_pos, 1)

            for s, n in ((d_lo, CREDIT_DOWN), (ht_lo, CREDIT_DOWN), (hd0, 1), (hd1, 1)):
                dve.sem_inc(s, n)

            def gu_split(q, value):
                dve.wait_ge(gu_hi, value)
                v.tensor_tensor(e_lo[:, q, :], e_raw[:, q, :], e_hi[:, q, :].bitcast(F32), ALU.subtract).then_inc(gu_lo, 1)

            def x_lo(slot, value):
                dve.wait_ge(xThi, value)
                v.tensor_tensor(xT_lo[:, slot, :], ps[:, 1, :], xT_hi[:, slot, :].bitcast(F32), ALU.subtract).then_inc(xTlo, 1)

            def hidden(half, n_sg, n_ah, done):
                dve.wait_ge(sgd, n_sg)
                pair_ps = ps[:, 0, half * F:(half + 1) * F]
                v.tensor_tensor(hid[:, half, :], pair_ps[:, 0:F // 2], sg[:, half, :], ALU.mult).then_inc(a_h, 1)
                dve.wait_ge(a_h, n_ah)
                v.tensor_tensor(hid[:, half, :], pair_ps[:, F // 2:F], hid[:, half, :], ALU.mult).then_inc(done, 1)

            def h_lo(half, value):
                dve.wait_ge(ht_hi, value)
                v.tensor_tensor(hT_lo[:, 2 * half:2 * half + 2, :], ps[:, 3, half * 4 * P:half * 4 * P + 2 * P],
                                hT_hi[:, 2 * half:2 * half + 2, :].bitcast(F32), ALU.subtract).then_inc(ht_lo, 1)

            n_blk = dve.value_load(tab[0:1, NBLK:NBLK + 1], min_val=1, max_val=NBLK - 1)
            for q in range(2):
                gu_split(q, q + 1)
            x_lo(0, 1)
            for q in range(2, 4):
                gu_split(q, q + 1)
            with dve.Fori(0, NBLK // 2) as pair:
                for s in range(2):
                    with dve.If(pair * 2 + s < n_blk):
                        b = pair * 2 + s
                        for q in range(2):
                            dve.wait_ge(d_hi, b * 2 + (q + 1))
                            v.tensor_tensor(e_lo[:, 4 + q, :], e_raw[:, 4 + q, :], e_hi[:, 4 + q, :].bitcast(F32),
                                            ALU.subtract).then_inc(d_lo, 1)
                        hidden(0, b * 2 + 1, b * 2 + 1, hd0)
                        h_lo(0, b * 2 + 1)
                        gu_split(0, b * 4 + 5)
                        hidden(1, b * 2 + 2, b * 2 + 2, hd1)
                        gu_split(1, b * 4 + 6)
                        h_lo(1, b * 2 + 2)
                        x_lo(1 - s, b + 2)
                        gu_split(2, b * 4 + 7)
                        gu_split(3, b * 4 + 8)

            for i in range(NT):
                dve.wait_ge(f_ssq, i + 1)
                step(rms(2, i))
                dve.wait_ge(s_g2_in, 16)
                if i >= 4:
                    dve.wait_ge(f_st[i % 4], 16)
                v.scalar_tensor_tensor(f_o[:, i % 4, :], f_x[i // 4][:, i % 4, :], rstd[:, i:i + 1], rows[:, SH2, :],
                                       ALU.mult, ALU.mult).then_inc(f_out, 1)

        @block.tensor
        def _(pe):
            t = nc.tensor

            def three(dst, st_hi, st_lo, mv_hi, mv_lo, first, last):
                t.matmul(dst, st_hi, mv_hi, start=first, stop=False)
                t.matmul(dst, st_hi, mv_lo, start=False, stop=False)
                return t.matmul(dst, st_lo, mv_hi, start=False, stop=last)

            pe.sem_inc(pe_slab, CREDIT_SLAB)
            pe.wait_ge(s_fill, 2)
            pe.wait_ge(s_par, 16 * 8)
            for k in range(KT):
                last = t.transpose(ps[:, 2, k * N_ROWS:(k + 1) * N_ROWS], prow[0:N_ROWS, k * P:(k + 1) * P], ident[0:N_ROWS, 0:N_ROWS])
            last.then_inc(s_parT, 1)
            for i in range(NT):
                pe.wait_ge(s_xn, i + 1)
                if i >= 2:
                    pe.wait_ge(s_xTev, i - 1)
                for k in range(KT):
                    last = t.transpose(ps[:, i % 2, k * P:(k + 1) * P], xn[:, i, k * P:(k + 1) * P], ident[:])
                last.then_inc(s_xT, 1)
            pe.wait_ge(s_macc, 1)
            pe.wait_ge(s_const, 1)
            for q in range(2):
                for k in range(KT):
                    last = t.matmul(ps[:, 3, q * KT + k:q * KT + k + 1], macc1[:, q, k * P:(k + 1) * P], ones[:, 0:1], start=True, stop=True)
            last.then_inc(s_modc, 1)

            def slab_product(slot, dst, k_ready=None):
                for k in range(KT):
                    if k_ready is not None:
                        pe.wait_ge(k_ready, k + 1)
                    for h in range(2):
                        cols_h = slice(h * H, (h + 1) * H)
                        last = three(dst[:, cols_h], w_hi[:, slot, k * P:(k + 1) * P], w_lo[:, slot, k * P:(k + 1) * P],
                                     A_hi[:, k, cols_h], A_lo[:, k, cols_h], k == 0, k == KT - 1)
                return last

            PS_FREE = {
                0: (dve_evac, 3, CREDIT_DVE_EVAC + 0), 1: (act_evac, 4, CREDIT_ACT_EVAC - 1), 2: (act_evac, 4, CREDIT_ACT_EVAC + 0),
                3: (dve_evac, 3, CREDIT_DVE_EVAC - 1), 4: (act_evac, 4, CREDIT_ACT_EVAC + 1), 5: (dve_evac, 3, CREDIT_DVE_EVAC + 1),
                6: (act_evac, 4, CREDIT_ACT_EVAC + 2)}
            with pe.Fori(0, KT) as ch:
                for kind in range(NK):
                    s, per, off = PS_FREE[kind]
                    pe.wait_ge(s, ch * per + off)
                    pe.wait_ge(w_lo_done, ch * NK + (kind + 1 + CREDIT_SLAB))
                    slab_product(W_SLOT[kind], ps[:, PS_SLOT[kind], :], s_hlo if kind == 0 else None).then_inc(pe_slab, 1)

            n0 = NK * KT

            def statistic(dst, src, ready, done):
                for k in range(KT):
                    pe.wait_ge(ready, k + 1)
                    for h in range(2):
                        last = t.matmul(dst[:, h * H:(h + 1) * H], mean_w[:], src(k, h), start=(k == 0), stop=(k == KT - 1))
                last.then_inc(done, 1)

            pe.wait_ge(act_evac, CREDIT_ACT_EVAC + 4 * KT)
            pe.wait_ge(dve_evac, CREDIT_DVE_EVAC + 3 * KT)
            for j in range(KT):
                slot, _, _ = slab_turn(n0 + j)
                pe.wait_ge(w_lo_done, n0 + j + 1 + CREDIT_SLAB)
                if j >= 2:
                    pe.wait_ge(s_ma, j - 1)
                slab_product(slot, ps[:, j % 2, :], s_alo if j == 0 else None).then_inc(pe_slab, 1)
                if j == 1:
                    statistic(ps[:, 2, :], lambda k, h: conf[:, k * S + h * H:k * S + (h + 1) * H], s_conf, s_mean)
                if j == 4:
                    statistic(ps[:, 3, :], lambda k, h: conf_sq[:, k, h * H:(h + 1) * H], s_sq, s_var)

            def rows_sum(q, slot):
                for h in range(2):
                    last = t.matmul(ps[:, slot, h * H:(h + 1) * H], ones[:], rows[:, q, h * H:(h + 1) * H], start=True, stop=True)
                last.then_inc(s_bc, 1)

            for j in range(KT):
                slot, _, _ = slab_turn(n0 + KT + j)
                pe.wait_ge(w_lo_done, n0 + KT + j + 1 + CREDIT_SLAB)
                if j < 2:
                    pe.wait_ge(s_ma, KT - 1 + j)
                else:
                    pe.wait_ge(ev2, j - 1)
                for k in range(KT):
                    if j == 0:
                        pe.wait_ge(s_blo, k + 1)
                    for h in range(2):
                        ch_ = slice(h * H, (h + 1) * H)
                        last = three(ps[:, j % 2, ch_], w_hi[:, slot, k * P:(k + 1) * P], w_lo[:, slot, k * P:(k + 1) * P],
                                     B_hi[:, k, ch_], B_lo[:, k, ch_], k == 0, k == KT - 1)
                last.then_inc(pe_slab, 1)
                if j == 1:
                    rows_sum(GT1, 2)
                    rows_sum(SH2, 3)
                if j == 3:
                    pe.wait_ge(s_bcev, 2)
                    rows_sum(A2, 2)
                    rows_sum(GT2, 3)

            def h2_transpose(i):
                pe.wait_ge(s_h2, i + 1)
                if i == 0:
                    pe.wait_ge(s_bcdv, 1)
                else:
                    pe.wait_ge(s_h2Tc, i)
                for k in range(KT):
                    last = t.transpose(ps[:, 2, k * P:(k + 1) * P], h2[:, i % 2, k * P:(k + 1) * P], ident[:])
                last.then_inc(s_h2T, 1)

            def router(i):
                pe.wait_ge(s_h2Tc, i + 1)
                pe.wait_ge(s_wr_in, 64)
                if i == 0:
                    pe.wait_ge(s_bcev, 3)
                else:
                    pe.wait_ge(s_lgev, i)
                for k in range(KT):
                    last = t.matmul(ps[:, 3, 0:NR], s2[:, k * P:(k + 1) * P], w_r[:, k, :], start=(k == 0), stop=(k == KT - 1))
                last.then_inc(s_lg, 1)

            pe.wait_ge(s_mlo, KT)
            for i in range(NT):
                pe.wait_ge(ev2, KT - 1 + i)
                for k in range(KT):
                    if i == 0:
                        pe.wait_ge(s_olo, k + 1)
                    for h in range(2):
                        ch_ = slice(h * H, (h + 1) * H)
                        last = three(ps[:, i % 2, ch_], A_hi[:, k, i * P:(i + 1) * P], A_lo[:, k, i * P:(i + 1) * P],
                                     B_hi[:, k, ch_], B_lo[:, k, ch_], k == 0, k == KT - 1)
                last.then_inc(pe_o, 1)
                if i >= 2:
                    router(i - 2)
                if i >= 1:
                    h2_transpose(i - 1)
            router(NT - 2)
            h2_transpose(NT - 1)
            router(NT - 1)
            pe.wait_ge(s_mask, 1)
            pe.wait_ge(ev2, KT + NT)
            t.matmul(ps[:, 0, 0:NT * NE], tri[:], mask[:].rearrange("p i e -> p (i e)"), start=True, stop=False)
            t.matmul(ps[:, 0, 0:NT * NE], ones[:], cum[:, 0:NT, :].rearrange("p i e -> p (i e)"), start=False, stop=True)
            t.matmul(ps[0:NE, 1, 0:1], cum[:, NT, :], ones[:, 0:1], start=True, stop=True).then_inc(s_rank, 1)
            pe.wait_ge(s_nb, 1)
            t.matmul(ps[:, 3, 0:NE], nb_b[:], tri[0:NE, 0:NE], start=True, stop=True).then_inc(s_start, 1)
            t.matmul(ps[0:NE, 3, H:H + 1], tri_i[0:NE, 0:NE], nb_e[:], start=True, stop=True).then_inc(s_pend, 1)

            def inverse(k):
                pe.wait_ge(s_ohr, k + 1)
                for i in range(NT):
                    last = t.matmul(ps[:, 2, 0:2 * NBLK], oh_r[:, k, i, :], inv_b[:, k, i].rearrange("p c b -> p (c b)"),
                                    start=(k == 0 and i == 0), stop=(k == 1 and i == NT - 1))
                return last

            inverse(0)
            pe.wait_ge(s_cmp, 1)
            t.matmul(ps[0:1, 1, H:H + NBLK + 1], ones[0:NE, 0:1], cmp_b[:], start=True, stop=True).then_inc(s_tabp, 1)
            inverse(1).then_inc(s_inv, 1)

            for s, n in ((t_done, 1), (d_used, CREDIT_DOWN)):
                pe.sem_inc(s, n)
            pe.wait_ge(s_pos, 1)

            def rows_transpose(slot):
                for k in range(KT):
                    last = t.transpose(ps[:, 1, k * P:(k + 1) * P], xg[:, slot, k * P:(k + 1) * P], ident[:])
                last.then_inc(t_done, 1)

            def hidden_transpose(half):
                for f in range(2):
                    last = t.transpose(ps[:, 3, half * 4 * P + f * P:half * 4 * P + (f + 1) * P], hid[:, half, f * P:(f + 1) * P], ident[:])
                last.then_inc(ht_ps, 1)

            def gate_up(half, slot, b):
                dst = ps[:, 0, half * F:(half + 1) * F].rearrange("p (w n) -> p w n", w=2)
                for q in range(4):
                    if half == 0:
                        pe.wait_ge(gu_lo, b * 4 + (q + 1))
                    for kk in range(2):
                        k = 2 * q + kk

                        def part(buf):
                            return buf[:, q, kk * D:(kk + 1) * D].rearrange("p (w n) -> p w n", w=2)[:, :, half * F // 2:(half + 1) * F // 2]
                        last = three(dst, xT_hi[:, slot, k * P:(k + 1) * P], xT_lo[:, slot, k * P:(k + 1) * P],
                                     part(e_hi), part(e_lo), k == 0, k == KT - 1)
                    if half == 1:
                        last.then_inc(gu_used, 1)
                        if q == 2:
                            pe.wait_ge(hd0, b + 2)
                            pe.wait_ge(ht_lo, b * 2 + (CREDIT_DOWN - 1))
                            hidden_transpose(0)
                if half == 0:
                    last.then_inc(gu0, 1)

            def down(f):
                q, kk = f // 2, f % 2
                for h in range(2):
                    ch_ = slice(kk * D + h * H, kk * D + (h + 1) * H)
                    last = three(ps[:, 2, h * H:(h + 1) * H], hT_hi[:, f, :], hT_lo[:, f, :],
                                 e_hi[:, 4 + q, ch_], e_lo[:, 4 + q, ch_], f == 0, f == FT - 1)
                if kk == 1:
                    last.then_inc(d_used, 1)

            n_blk = pe.value_load(tab[0:1, NBLK:NBLK + 1], min_val=1, max_val=NBLK - 1)
            pe.wait_ge(xg_full[0], 16)
            rows_transpose(0)
            with pe.Fori(0, NBLK // 2) as pair:
                for s in range(2):
                    with pe.If(pair * 2 + s < n_blk):
                        b = pair * 2 + s
                        pe.wait_ge(xTlo, b + 1)
                        pe.wait_ge(hd0, b + 1)
                        gate_up(0, s, b)
                        pe.wait_ge(hd1, b + 1)
                        gate_up(1, s, b)
                        pe.wait_ge(ht_lo, b * 2 + (1 + CREDIT_DOWN))
                        pe.wait_ge(d_lo, b * 2 + (1 + CREDIT_DOWN))
                        pe.wait_ge(y_ev, b + 1)
                        down(0)
                        down(1)
                        pe.wait_ge(hd1, b + 2)
                        hidden_transpose(1)
                        pe.wait_ge(xg_full[1 - s], pair * 16 + 16 * (1 + s))
                        rows_transpose(1 - s)
                        pe.wait_ge(ht_lo, b * 2 + (2 + CREDIT_DOWN))
                        pe.wait_ge(d_lo, b * 2 + (2 + CREDIT_DOWN))
                        down(2)
                        down(3)


_INS = ["x", "c", "w_ada", "b_ada", "g_norm1", "w_in", "conv_a", "w_a_out", "conv_b", "b_conv_b", "ln_conv_g", "ln_conv_b",
        "w_b_out", "w_o", "g_norm2", "w_router_g", "b_router_g", "w_router_e", "b_router_e", "w_gate", "w_up", "w_down", "g_final"]


def kernel(**inputs):
    import concourse.bacc as _bacc
    from concourse.bass_utils import run_bass_kernel_spmd as _run

    nc = _bacc.Bacc("TRN2", target_bir_lowering=False, num_devices=1)
    arrays, args = {}, []
    for name in _INS:
        a = np.ascontiguousarray(inputs[name])
        if name == "b_ada":
            a = a.reshape(6, -1)
        elif name == "g_final":
            a = a.reshape(1, -1)
        elif a.ndim >= 3 or name in ("w_ada", "w_in"):
            a = a.reshape(a.shape[1:])
        arrays[f"in_{name}_dram"] = a
        args.append(nc.dram_tensor(f"in_{name}_dram", a.shape, mybir.dt.from_np(a.dtype), kind="ExternalInput").ap())
    S, D = arrays["in_x_dram"].shape
    args.append(nc.dram_tensor("out_0_dram", (S, D), F32, kind="ExternalOutput").ap())
    encoder_block(nc, *args)
    r = _run(nc, [arrays], core_ids=[0])
    return r.results[0]["out_0_dram"].reshape(1, S, D)
```
